# Optimizing a Trainium2 kernel written in Bass

```python
import jax, jax.numpy as jnp
from jax import lax
import numpy as np

D_MODEL = 1024
BATCH = 1
SEQ = 1024
DEPTH = 1

CHUNK = 64
Q_BLOCK = 128
SB_HEADS = 8
SB_HEAD_DIM = D_MODEL // SB_HEADS
SB_WIDTH = SB_HEADS * SB_HEAD_DIM
RET_HEADS = 4
RET_KEY_DIM = D_MODEL // RET_HEADS
RET_VAL_DIM = D_MODEL // RET_HEADS
RET_QK_WIDTH = RET_HEADS * RET_KEY_DIM
RET_WIDTH = RET_HEADS * RET_VAL_DIM
ROPE_BASE = 10000.0
EPS = 1e-6
SPLIT_SIZES = (SB_WIDTH, SB_WIDTH, SB_WIDTH, SB_WIDTH,
               RET_QK_WIDTH, RET_QK_WIDTH, RET_WIDTH, RET_WIDTH,
               D_MODEL, D_MODEL)
IN_COLS = sum(SPLIT_SIZES)
SPLIT_POINTS = tuple(int(v) for v in np.cumsum(SPLIT_SIZES)[:-1])


def rms_norm(x, gain):
    xf = x.astype(jnp.float32)
    y = xf * lax.rsqrt(jnp.mean(xf * xf, axis=-1, keepdims=True) + EPS)
    return (y * gain.astype(jnp.float32)).astype(x.dtype)

def split_heads(t, n_heads):
    b, s, w = t.shape
    return t.reshape(b, s, n_heads, w // n_heads).transpose(0, 2, 1, 3)

def merge_heads(t):
    b, h, s, d = t.shape
    return t.transpose(0, 2, 1, 3).reshape(b, s, h * d)

def rotary(t):
    s, d = t.shape[2], t.shape[3]
    inv_freq = ROPE_BASE ** (-jnp.arange(0, d, 2, dtype=jnp.float32) / d)
    ang = jnp.arange(s, dtype=jnp.float32)[:, None] * inv_freq[None, :]
    cos, sin = jnp.cos(ang), jnp.sin(ang)
    tf = t.astype(jnp.float32)
    t1, t2 = tf[..., : d // 2], tf[..., d // 2:]
    out = jnp.concatenate([t1 * cos - t2 * sin, t1 * sin + t2 * cos], axis=-1)
    return out.astype(t.dtype)

def stick_breaking_attention(q, k, v):
    b, h, s, d = q.shape
    nb = s // Q_BLOCK
    qb = q.reshape(b, h, nb, Q_BLOCK, d).transpose(2, 0, 1, 3, 4)
    kpos = jnp.arange(s)
    scale = d ** -0.5

    def block(args):
        qi, i = args
        z = jnp.einsum('bhqd,bhkd->bhqk', qi, k).astype(jnp.float32) * scale
        qpos = i * Q_BLOCK + jnp.arange(Q_BLOCK)
        mask = kpos[None, :] < qpos[:, None]
        log_keep = jnp.where(mask, jax.nn.log_sigmoid(-z), 0.0)
        suffix = lax.cumsum(log_keep, axis=3, reverse=True) - log_keep
        w = jnp.where(mask, jnp.exp(jax.nn.log_sigmoid(z) + suffix), 0.0)
        return jnp.einsum('bhqk,bhkd->bhqd', w.astype(v.dtype), v)

    out = lax.map(block, (qb, jnp.arange(nb)))
    return out.transpose(1, 2, 0, 3, 4).reshape(b, h, s, d)

def chunkwise_retention(q, k, v):
    dtype = v.dtype
    q, k, v = (a.astype(jnp.float32) for a in (q, k, v))
    b, h, s, dk = q.shape
    dv = v.shape[-1]
    n = s // CHUNK
    log_gamma = jnp.log1p(-jnp.exp2(-5.0 - jnp.arange(h, dtype=jnp.float32)))
    qc = q.reshape(b, h, n, CHUNK, dk)
    kc = k.reshape(b, h, n, CHUNK, dk)
    vc = v.reshape(b, h, n, CHUNK, dv)
    idx = jnp.arange(CHUNK, dtype=jnp.float32)
    intra_decay = jnp.exp(log_gamma[:, None, None] * jnp.abs(idx[:, None] - idx[None, :]))
    scores = jnp.einsum('bhnqd,bhnkd->bhnqk', qc, kc) * intra_decay[None, :, None]
    intra = jnp.einsum('bhnqk,bhnke->bhnqe', scores, vc)
    q_decay = jnp.exp(log_gamma[:, None] * (idx + 1.0))[None, :, :, None]
    k_decay = jnp.exp(log_gamma[:, None] * (CHUNK - 1.0 - idx))[None, :, :, None]
    chunk_decay = jnp.exp(log_gamma * CHUNK)[None, :, None, None]

    def step(state, inp):
        qi, ki, vi = inp
        out = jnp.einsum('bhqd,bhde->bhqe', qi * q_decay, state)
        state = state * chunk_decay + jnp.einsum('bhkd,bhke->bhde', ki * k_decay, vi)
        return state, out

    init = jnp.zeros((b, h, dk, dv), jnp.float32)
    xs = (qc.transpose(2, 0, 1, 3, 4), kc.transpose(2, 0, 1, 3, 4), vc.transpose(2, 0, 1, 3, 4))
    _, inter = lax.scan(step, init, xs)
    out = intra + inter.transpose(1, 2, 0, 3, 4)
    return out.reshape(b, h, s, dv).astype(dtype)

def first_inputs(seed: int = 0) -> dict:
    key = jax.random.key(seed)
    ks = jax.random.split(key, 10)
    f32 = jnp.float32
    x = jax.random.normal(ks[0], (BATCH, SEQ, D_MODEL), f32)
    norm_gain = 1.0 + 0.05 * jax.random.normal(ks[1], (DEPTH, D_MODEL), f32)
    w_in = jax.random.normal(ks[2], (DEPTH, D_MODEL, IN_COLS), f32) * D_MODEL ** -0.5
    b_merge = 0.01 * jax.random.normal(ks[3], (DEPTH, 2, D_MODEL), f32)
    sb_q_gain = 1.0 + 0.05 * jax.random.normal(ks[4], (DEPTH, SB_HEAD_DIM), f32)
    sb_k_gain = 1.0 + 0.05 * jax.random.normal(ks[5], (DEPTH, SB_HEAD_DIM), f32)
    ret_out_gain = 1.0 + 0.05 * jax.random.normal(ks[6], (DEPTH, RET_HEADS, RET_VAL_DIM), f32)
    w_branch_sb = jax.random.normal(ks[7], (DEPTH, SB_WIDTH, D_MODEL), f32) * SB_WIDTH ** -0.5
    w_branch_ret = jax.random.normal(ks[8], (DEPTH, RET_WIDTH, D_MODEL), f32) * RET_WIDTH ** -0.5
    w_out = jax.random.normal(ks[9], (DEPTH, D_MODEL, D_MODEL), f32) * D_MODEL ** -0.5
    return {"x": x, "norm_gain": norm_gain, "w_in": w_in, "b_merge": b_merge,
            "sb_q_gain": sb_q_gain, "sb_k_gain": sb_k_gain, "ret_out_gain": ret_out_gain,
            "w_branch_sb": w_branch_sb, "w_branch_ret": w_branch_ret, "w_out": w_out}

def first_block(x, norm_gain, w_in, b_merge, sb_q_gain, sb_k_gain, ret_out_gain,
              w_branch_sb, w_branch_ret, w_out):
    for layer in range(DEPTH):
        h = rms_norm(x, norm_gain[layer])
        proj = jnp.einsum('bsd,dc->bsc', h, w_in[layer])
        (sb_q, sb_k, sb_v, sb_g, r_q, r_k, r_v, r_g, m_sb, m_ret) = jnp.split(proj, SPLIT_POINTS, axis=-1)

        qa = rms_norm(split_heads(sb_q, SB_HEADS), sb_q_gain[layer])
        ka = rms_norm(split_heads(sb_k, SB_HEADS), sb_k_gain[layer])
        va = split_heads(sb_v, SB_HEADS)
        out_a = merge_heads(stick_breaking_attention(qa, ka, va)) * jax.nn.silu(sb_g)

        qb = rotary(split_heads(r_q, RET_HEADS))
        kb = rotary(split_heads(r_k, RET_HEADS)) * (RET_KEY_DIM ** -0.5)
        vb = split_heads(r_v, RET_HEADS)
        ret = chunkwise_retention(qb, kb, vb)
        ret = rms_norm(ret, ret_out_gain[layer][None, :, None, :])
        out_b = merge_heads(ret) * jax.nn.silu(r_g)

        p_a = jnp.einsum('bsw,wd->bsd', out_a, w_branch_sb[layer])
        p_b = jnp.einsum('bsw,wd->bsd', out_b, w_branch_ret[layer])
        merged = (jax.nn.sigmoid(m_sb + b_merge[layer, 0]) * p_a
                  + jax.nn.sigmoid(m_ret + b_merge[layer, 1]) * p_b)
        x = x + jnp.einsum('bsd,de->bse', merged, w_out[layer])
    return x


N_META = 16
D_MIX = D_MODEL
GLA_HEADS = 4
GLA_DK = D_MIX // 4 // GLA_HEADS
GLA_DV = D_MIX // 2 // GLA_HEADS
GLA_RANK = 16
GLA_TAU = 16.0
GLA_CHUNK = 64
GLA_PAD = GLA_CHUNK - N_META
SWA_HEADS = 8
SWA_KV_HEADS = 2
SWA_GROUP = SWA_HEADS // SWA_KV_HEADS
SWA_HD = D_MIX // 2 // SWA_HEADS
SWA_WINDOW = 128
SWA_BLOCK = 128
ROPE_DIM = SWA_HD // 4
ROPE_THETA = 500000.0
D_FF = 4 * D_MODEL
EPS_2 = 1e-5

IN_SIZES = (GLA_HEADS * GLA_DK,
            GLA_HEADS * GLA_DK,
            GLA_HEADS * GLA_DV,
            GLA_HEADS * GLA_DV,
            GLA_RANK,
            SWA_HEADS * SWA_HD,
            SWA_KV_HEADS * SWA_HD,
            SWA_KV_HEADS * SWA_HD)
D_IN = sum(IN_SIZES)


def rmsnorm(x, w):
    xf = x.astype(jnp.float32)
    y = xf * lax.rsqrt(jnp.mean(jnp.square(xf), axis=-1, keepdims=True) + EPS_2)
    return (y * w.astype(jnp.float32)).astype(x.dtype)

def partial_rope(x, pos):
    inv_freq = 1.0 / (ROPE_THETA ** (jnp.arange(0, ROPE_DIM, 2, dtype=jnp.float32) / ROPE_DIM))
    ang = pos.astype(jnp.float32)[:, None] * inv_freq[None, :]
    ang = jnp.concatenate([ang, ang], axis=-1)[:, None, :]
    cos, sin = jnp.cos(ang), jnp.sin(ang)
    xr = x[..., :ROPE_DIM].astype(jnp.float32)
    half = ROPE_DIM // 2
    rot = jnp.concatenate([-xr[..., half:], xr[..., :half]], axis=-1)
    xr = (xr * cos + rot * sin).astype(x.dtype)
    return jnp.concatenate([xr, x[..., ROPE_DIM:]], axis=-1)

def gla_chunk_step(S, inp):
    q, k, v, g = inp
    b = jnp.cumsum(g, axis=2)
    causal = jnp.tril(jnp.ones((GLA_CHUNK, GLA_CHUNK), dtype=bool))
    diff = b[:, :, :, None, :] - b[:, :, None, :, :]
    decay = jnp.exp(jnp.where(causal[None, None, :, :, None], diff, -jnp.inf))
    A = jnp.einsum('bhid,bhjd,bhijd->bhij', q, k, decay)
    o = (jnp.einsum('bhij,bhjv->bhiv', A, v)
         + jnp.einsum('bhid,bhdv->bhiv', q * jnp.exp(b), S))
    b_last = b[:, :, -1:, :]
    S = (jnp.exp(b_last[:, :, 0, :])[..., None] * S
         + jnp.einsum('bhjd,bhjv->bhdv', k * jnp.exp(b_last - b), v))
    return S, o

def gla_mixer(q, k, v, r, lr, w_gate_up, b_gate, gla_norm_w):
    B, L, _ = q.shape
    dtype = q.dtype
    g = jax.nn.log_sigmoid((lr @ w_gate_up + b_gate).astype(jnp.float32)) / GLA_TAU
    q = q.astype(jnp.float32).reshape(B, L, GLA_HEADS, GLA_DK) * (GLA_DK ** -0.5)
    k = k.astype(jnp.float32).reshape(B, L, GLA_HEADS, GLA_DK)
    v = v.astype(jnp.float32).reshape(B, L, GLA_HEADS, GLA_DV)
    g = g.reshape(B, L, GLA_HEADS, GLA_DK)
    pad = ((0, 0), (GLA_PAD, 0), (0, 0), (0, 0))
    Lp = L + GLA_PAD
    n_chunks = Lp // GLA_CHUNK

    def to_chunks(t):
        t = jnp.pad(t, pad).reshape(B, n_chunks, GLA_CHUNK, GLA_HEADS, t.shape[-1])
        return t.transpose(1, 0, 3, 2, 4)

    S0 = jnp.zeros((B, GLA_HEADS, GLA_DK, GLA_DV), jnp.float32)
    _, o = lax.scan(gla_chunk_step, S0, (to_chunks(q), to_chunks(k), to_chunks(v), to_chunks(g)))
    o = o.transpose(1, 0, 3, 2, 4).reshape(B, Lp, GLA_HEADS, GLA_DV)[:, GLA_PAD:]
    o = rmsnorm(o.astype(dtype), gla_norm_w)
    o = o * jax.nn.silu(r.reshape(B, L, GLA_HEADS, GLA_DV))
    return o.reshape(B, L, GLA_HEADS * GLA_DV)

def sink_softmax(scores, sink):
    sink_b = jnp.broadcast_to(sink, scores.shape[:-1] + (1,))
    p = jax.nn.softmax(jnp.concatenate([scores, sink_b], axis=-1), axis=-1)
    return p[..., :-1]

def swa_mixer(q, k, v, sinks, pos):
    B, L, _ = q.shape
    dtype = q.dtype
    q = partial_rope(q.reshape(B, L, SWA_HEADS, SWA_HD), pos) * (SWA_HD ** -0.5)
    k = partial_rope(k.reshape(B, L, SWA_KV_HEADS, SWA_HD), pos)
    v = v.reshape(B, L, SWA_KV_HEADS, SWA_HD)
    q = q.reshape(B, L, SWA_KV_HEADS, SWA_GROUP, SWA_HD)
    qm, qr = q[:, :N_META], q[:, N_META:]
    km, kr = k[:, :N_META], k[:, N_META:]
    vm, vr = v[:, :N_META], v[:, N_META:]
    sink = sinks.astype(jnp.float32).reshape(SWA_KV_HEADS, SWA_GROUP)

    sm = jnp.einsum('bqkgd,bjkd->bkgqj', qm, km).astype(jnp.float32)
    mmask = jnp.tril(jnp.ones((N_META, N_META), dtype=bool))
    pm = sink_softmax(jnp.where(mmask, sm, -jnp.inf), sink[None, :, :, None, None])
    om = jnp.einsum('bkgqj,bjkd->bqkgd', pm.astype(dtype), vm).reshape(B, N_META, SWA_HEADS * SWA_HD)

    S = L - N_META
    nb = S // SWA_BLOCK
    qb = qr.reshape(B, nb, SWA_BLOCK, SWA_KV_HEADS, SWA_GROUP, SWA_HD)

    def band(t):
        cur = t.reshape(B, nb, SWA_BLOCK, SWA_KV_HEADS, SWA_HD)
        prev = jnp.pad(t, ((0, 0), (SWA_BLOCK, 0), (0, 0), (0, 0)))[:, :S]
        prev = prev.reshape(B, nb, SWA_BLOCK, SWA_KV_HEADS, SWA_HD)
        return jnp.concatenate([prev, cur], axis=2)

    kw, vw = band(kr), band(vr)
    s_meta = jnp.einsum('bnqkgd,bjkd->bnkgqj', qb, km).astype(jnp.float32)
    s_win = jnp.einsum('bnqkgd,bnjkd->bnkgqj', qb, kw).astype(jnp.float32)
    rr = jnp.arange(SWA_BLOCK)[:, None]
    jj = jnp.arange(2 * SWA_BLOCK)[None, :]
    dist = SWA_BLOCK + rr - jj
    in_band = (dist >= 0) & (dist < SWA_WINDOW)
    blk = jnp.arange(nb)[:, None, None]
    wmask = in_band[None] & ((blk > 0) | (jj[None] >= SWA_BLOCK))
    s_win = jnp.where(wmask[None, :, None, None], s_win, -jnp.inf)
    p = sink_softmax(jnp.concatenate([s_meta, s_win], axis=-1),
                     sink[None, None, :, :, None, None]).astype(dtype)
    orr = (jnp.einsum('bnkgqj,bjkd->bnqkgd', p[..., :N_META], vm)
           + jnp.einsum('bnkgqj,bnjkd->bnqkgd', p[..., N_META:], vw))
    orr = orr.reshape(B, S, SWA_HEADS * SWA_HD)
    return jnp.concatenate([om, orr], axis=1)

def hybrid_layer(h, pos, norm_mix_w, w_in, w_gate_up, b_gate, gla_norm_w, sinks,
                 w_out, norm_ff_w, w_ff1, w_ff2):
    u = rmsnorm(h, norm_mix_w)
    proj = u @ w_in
    split_points = np.cumsum(IN_SIZES)[:-1].tolist()
    gq, gk, gv, gr, glr, sq, sk, sv = jnp.split(proj, split_points, axis=-1)
    o_gla = gla_mixer(gq, gk, gv, gr, glr, w_gate_up, b_gate, gla_norm_w)
    o_swa = swa_mixer(sq, sk, sv, sinks, pos)
    h = h + jnp.concatenate([o_gla, o_swa], axis=-1) @ w_out
    f = rmsnorm(h, norm_ff_w)
    return h + jnp.square(jax.nn.relu(f @ w_ff1)) @ w_ff2

def second_inputs(seed: int = 0) -> dict:
    key = jax.random.key(seed)
    ks = jax.random.split(key, 14)
    f32 = jnp.float32
    nrm = lambda k, shape, s: jax.random.normal(k, shape, f32) * s
    return {
        "x": nrm(ks[0], (BATCH, SEQ, D_MODEL), 1.0),
        "meta_tokens": nrm(ks[1], (N_META, D_MODEL), 1.0),
        "norm_mix_w": 1.0 + nrm(ks[2], (DEPTH, D_MODEL), 0.02),
        "w_in": nrm(ks[3], (DEPTH, D_MODEL, D_IN), D_MODEL ** -0.5),
        "w_gate_up": nrm(ks[4], (DEPTH, GLA_RANK, GLA_HEADS * GLA_DK), GLA_RANK ** -0.5),
        "b_gate": nrm(ks[5], (DEPTH, GLA_HEADS * GLA_DK), 0.1),
        "gla_norm_w": 1.0 + nrm(ks[6], (DEPTH, GLA_DV), 0.02),
        "sinks": nrm(ks[7], (DEPTH, SWA_HEADS), 1.0),
        "w_out": nrm(ks[8], (DEPTH, D_MIX, D_MODEL), D_MIX ** -0.5),
        "norm_ff_w": 1.0 + nrm(ks[9], (DEPTH, D_MODEL), 0.02),
        "w_ff1": nrm(ks[10], (DEPTH, D_MODEL, D_FF), D_MODEL ** -0.5),
        "w_ff2": nrm(ks[11], (DEPTH, D_FF, D_MODEL), D_FF ** -0.5),
        "final_norm_w": 1.0 + nrm(ks[12], (D_MODEL,), 0.02),
    }

def second_block(x, meta_tokens, norm_mix_w, w_in, w_gate_up, b_gate, gla_norm_w, sinks,
              w_out, norm_ff_w, w_ff1, w_ff2, final_norm_w):
    B = x.shape[0]
    meta = jnp.broadcast_to(meta_tokens[None].astype(x.dtype), (B, N_META, D_MODEL))
    h = jnp.concatenate([meta, x], axis=1)
    pos = jnp.arange(h.shape[1], dtype=jnp.int32)
    for layer in range(DEPTH):
        h = hybrid_layer(h, pos, norm_mix_w[layer], w_in[layer], w_gate_up[layer], b_gate[layer],
                         gla_norm_w[layer], sinks[layer], w_out[layer], norm_ff_w[layer],
                         w_ff1[layer], w_ff2[layer])
    return rmsnorm(h, final_norm_w)[:, N_META:]


def setup_inputs(seed=0):
    out = dict(first_inputs(seed))
    for name, value in second_inputs(seed + 1).items():
        if name != "x":
            out[name + "_2"] = value
    return out


def reference(
    x, norm_gain, w_in, b_merge, sb_q_gain, sb_k_gain, ret_out_gain, w_branch_sb, w_branch_ret,
    w_out, meta_tokens_2, norm_mix_w_2, w_in_2, w_gate_up_2, b_gate_2, gla_norm_w_2, sinks_2,
    w_out_2, norm_ff_w_2, w_ff1_2, w_ff2_2, final_norm_w_2,
):
    x = first_block(
        x, norm_gain, w_in, b_merge, sb_q_gain, sb_k_gain, ret_out_gain, w_branch_sb,
        w_branch_ret, w_out,
    )
    return second_block(
        x, meta_tokens_2, norm_mix_w_2, w_in_2, w_gate_up_2, b_gate_2, gla_norm_w_2, sinks_2,
        w_out_2, norm_ff_w_2, w_ff1_2, w_ff2_2, final_norm_w_2,
    )


_drawn_inputs = setup_inputs


def setup_inputs(seed=0):
    import zlib

    import numpy as np

    out = dict(_drawn_inputs(seed))
    spreads = {}
    factors = {'b_merge': 8.0,
     'sb_q_gain': 8.0,
     'sb_k_gain': 8.0,
     'ret_out_gain': 2.82,
     'norm_mix_w_2': 3.441,
     'b_gate_2': 3.183,
     'gla_norm_w_2': 6.839,
     'sinks_2': 64.0,
     'norm_ff_w_2': 10.416,
     'final_norm_w_2': 8.049}
    for name, (base, spread) in spreads.items():
        noise = np.random.default_rng([zlib.crc32(name.encode()), seed]).standard_normal(out[name].shape)
        drawn = base * np.exp(spread * noise) if base else spread * noise
        out[name] = __import__('jax').numpy.asarray(drawn.astype(out[name].dtype))
    for name, factor in factors.items():
        out[name] = (out[name] * factor).astype(out[name].dtype)
    return out
```

```python
import numpy as np
import concourse.bass as bass
from concourse import mybir
from contextlib import ExitStack

SEQ, DM = 1024, 1024
P = 128
KT = DM // P
TT = SEQ // P
HALF = 512
BC = 256
META = 16
NT = SEQ + META
SB_HEADS, RET_HEADS = 8, 4
GLA_LEVELS = (64, 32, 16, 8, 4, 2, 1, 0)
KEYS = 2 * P + META
NEG = -1.0e30
LOG_EXP = "natural_log_exp_and_others"
CLAMP = 40.0


def shape_tables():
    f = np.float32
    t = np.arange(SEQ, dtype=f)
    inv = (f(10000.0) ** (-np.arange(0, 256, 2, dtype=f) / f(256))).astype(f)
    ang = (inv[:, None] * t[None, :]).astype(f)
    tabs = {"rcos": np.cos(ang).astype(f), "rsin": np.sin(ang).astype(f)}
    lg = np.log1p(-np.exp2(-5.0 - np.arange(RET_HEADS, dtype=np.float64)))
    s, q = np.arange(P)[:, None], np.arange(SEQ)[None, :]
    keep = ~((s // 64 > q // 64) & (q < P))
    tabs["decay"] = np.stack([np.exp(g * np.abs(q - s)) * keep / 16.0 for g in lg]).astype(f)
    a, b = np.arange(P)[:, None], np.arange(P)[None, :]
    tabs["ident"] = (a == b).astype(f)
    tabs["causal"] = np.where(b < a, 0.0, NEG).astype(f)
    pos = np.arange(NT, dtype=f)
    inv2 = (f(1.0) / (f(500000.0) ** (np.arange(0, 16, 2, dtype=f) / f(16)))).astype(f)
    ang2 = (pos[None, :] * inv2[:, None]).astype(f)
    cos2, sin2 = np.ones((P, NT), f), np.zeros((P, NT), f)
    rot = np.zeros((P, P), f)
    for h in (0, 64):
        for d in range(16):
            cos2[h + d], sin2[h + d] = np.cos(ang2[d % 8]), np.sin(ang2[d % 8])
            rot[h + (d + 8) % 16, h + d] = -1.0 if d < 8 else 1.0
    tabs["pcos"], tabs["psin"], tabs["rot"] = cos2, sin2, rot
    dup = np.zeros((2, P, P), f)
    for g in range(2):
        for d in range(64):
            dup[g, g * 64 + d, d] = dup[g, g * 64 + d, 64 + d] = 1.0
    tabs["dup"] = dup
    j = np.arange(KEYS)[None, :]
    dist = P + a - j
    tabs["window"] = np.where((j >= 2 * P) | ((dist >= 0) & (dist < P)), 0.0, NEG).astype(f)
    lv = np.zeros((P, len(GLA_LEVELS), P), f)
    for n, w in enumerate(GLA_LEVELS):
        lv[:, n, :] = (a == b) if w == 0 else ((a // (2 * w) == b // (2 * w)) & (a % (2 * w) < w) & (b % (2 * w) >= w))
    tabs["levels"] = lv
    tabs["restart"] = np.broadcast_to((np.arange(SEQ) % P != 0).astype(f), (P, SEQ)).copy()
    return tabs


def build(nc, x, norm_gain, w_in, b_merge, sb_q_gain, sb_k_gain, ret_out_gain, w_branch_sb, w_branch_ret, w_out,
          meta_tokens_2, norm_mix_w_2, w_in_2, w_gate_up_2, b_gate_2, gla_norm_w_2, sinks_2, w_out_2,
          norm_ff_w_2, w_ff1_2, w_ff2_2, final_norm_w_2, tab, out):
    f32, f32r, i32 = mybir.dt.float32, mybir.dt.float32r, mybir.dt.int32
    ACT, ALU, AX = mybir.ActivationFunctionType, mybir.AluOpType, mybir.AxisListType
    ds = bass.ds

    cur = [-(-nc.sbuf_base // 64) * 64]

    def at(name, shape, dt=f32, off=None):
        size = int(np.prod(shape[1:])) * 4
        o = cur[0] if off is None else off
        t = nc.alloc_sbuf_tensor_at(name, shape, dt, offset=o)
        if off is None:
            cur[0] += size
        return t

    ident = at("ident", [P, P])
    ones = at("ones", [P, P])
    cols = at("cols", [P, 64])
    stats = at("stats", [P, 64])
    nb_at = cur[0]
    NB = [at(f"nb{j}", [P, HALF]) for j in range(4)]
    a_at = cur[0]
    A_hi = at("a_hi", [P, KT, NT], f32r)
    A_lo = at("a_lo", [P, KT, NT], f32r)
    W_hi = [at(f"w_hi{s}", [P, KT, BC], f32r) for s in range(2)]
    raw_at = [cur[0], cur[0] + KT * BC * 4]
    W_raw = [at(f"w_raw{s}", [P, KT, BC]) for s in range(2)]
    W_lo = [at(f"w_lo{s}", [P, KT, BC], f32r, off=raw_at[s]) for s in range(2)]
    out_at = cur[0]
    OUT = at("out_t", [P, KT, SEQ])
    X1 = at("x1", [P, TT, DM], off=out_at)
    work_at = cur[0]
    work_end = nc.sbuf_usable_end
    pos = [0]

    def work(name, shape, dt=f32):
        t = at(name, shape, dt, off=pos[0])
        pos[0] += int(np.prod(shape[1:])) * 4
        assert pos[0] <= work_end, (name, pos[0] - work_end)
        return t

    pos[0] = work_at
    XT = [work(f"xt{u}", [P, DM]) for u in range(4)]
    XS = [work(f"xs{u}", [P, DM]) for u in range(4)]
    G1 = work("g1", [P, DM])
    rows = work("rows", [32, P])
    pos[0] = work_at
    Q = work("q", [P, 2, SEQ])
    K = work("k", [P, 2, SEQ])
    V = work("v", [P, TT, BC])
    L = [work(f"l{u}", [P, SEQ]) for u in range(2)]
    R = [work(f"r{u}", [P, SEQ]) for u in range(2)]
    C = [work(f"c{u}", [P, SEQ]) for u in range(2)]
    WT = [work(f"wt{u}", [P, TT, 2 * P]) for u in range(2)]
    causal = work("causal", [P, P])
    pos[0] = work_at
    S_hi = work("s_hi", [P, KT, SEQ], f32r)
    S_lo = work("s_lo", [P, KT, SEQ], f32r)
    stage = [work(f"stage{u}", [P, HALF]) for u in range(2)]
    pos[0] = work_at
    RQ = work("rq", [P, 2, SEQ])
    RK = work("rk", [P, 2, SEQ])
    RV = work("rv", [P, TT, BC])
    rcos = work("rcos", [P, SEQ])
    rsin = work("rsin", [P, SEQ])
    decay = work("decay", [P, SEQ])
    AT = [work(f"at{u}", [P, SEQ]) for u in range(2)]
    RT = [work(f"rt{u}", [P, HALF]) for u in range(4)]
    pos[0] = work_at + 64 * 1024
    XB = [work(f"xb{u}", [P, 2, BC]) for u in range(2)]

    pos[0] = work_at
    SQ = work("sq", [P, 4, SEQ])
    SK = work("sk", [P, 2, NT])
    SV = work("sv", [P, TT, 2, 192])
    SVM = work("svm", [META, 2, 192])
    pcos = work("pcos", [P, NT])
    psin = work("psin", [P, NT])
    rot = work("rot", [P, P])
    dup = work("dup", [P, 2, P])
    window = work("window", [P, KEYS])
    sinks = work("sinks", [P, 8])
    sbuf_at = pos[0]
    SS = [work(f"ss{u}", [P, 4, KEYS]) for u in range(3)]
    SKR = at("skr", [P, NT], off=sbuf_at)
    PR = [work(f"pr{u}", [P, HALF]) for u in range(2)]
    SM = work("sm", [P, 3, 4, 4])
    KMT = work("kmt", [META, P])
    KMR = work("kmr", [P, META])
    PT = [[at(f"pt{u}{c}", [P, HALF], off=out_at + (3 * u + c) * HALF * 4) for c in range(3)] for u in range(2)]
    pos[0] = work_at
    GQ = work("gq", [P, 2, SEQ])
    GK = work("gk", [P, 2, NT])
    GB = work("gb", [P, 2, NT])
    GV = work("gv", [P, TT, 512])
    GVM = work("gvm", [META, 512])
    lr_at = pos[0]
    LR = work("lr", [16, NT])
    KTK = at("ktk", [P, TT, P], off=lr_at)
    wgu = work("wgu", [16, 256])
    lvl = work("lvl", [P, len(GLA_LEVELS), P])
    AA = work("aa", [P, TT * 2, P])
    e_at = pos[0]
    GE = work("ge", [P, SEQ])
    restart = work("restart", [P, SEQ])
    GS = [at(f"gs{u}", [P, 256], off=pos[0] - SEQ * 4 + u * 1024) for u in range(2)]
    KTM = at("ktm", [META, P], off=pos[0] - SEQ * 4 + 2048)
    GT = [at(f"gt{u}", [P, HALF], off=out_at + u * HALF * 4) for u in range(2)]
    QE = [at("qe0", [P, SEQ], off=out_at + 2 * SEQ * 4), at("qe1", [P, SEQ], off=nb_at)]
    KE = [at("ke0", [P, SEQ], off=out_at + 3 * SEQ * 4), at("ke1", [P, SEQ], off=nb_at + SEQ * 4)]
    GD = work("gd", [P, 16])
    KEM = work("kem", [P, META])
    pos[0] = work_at
    F_hi = work("f_hi", [P, KT, SEQ], f32r)
    F_lo = work("f_lo", [P, KT, SEQ], f32r)
    FS = [work(f"fs{u}", [P, HALF]) for u in range(2)]
    YB = [at(f"yb{u}", [P, DM], off=a_at + u * DM * 4) for u in range(4)]
    GF = at("gf", [P, DM], off=a_at + 4 * DM * 4)

    ctx = ExitStack()
    with ctx:
        ps = ctx.enter_context(nc.psum_tensor("ps", [P, 8, HALF], f32))
        bank = [ps[:, b, :] for b in range(8)]

        def wide(b, w=SEQ):
            return ps[:, b:b + 2, :].rearrange("p a b -> p (a b)")[:, 0:w]

        def sem(name):
            return ctx.enter_context(nc.semaphore(name))

        w_loaded = [sem(f"w_loaded{s}") for s in range(2)]
        w_hi, w_lo, gp_done = sem("w_hi_ready"), sem("w_lo_ready"), sem("gemm_output_done")
        kept = [sem(f"output{j}_kept") for j in range(4)]
        const_in, const_ok = sem("constants_in"), sem("constants_ok")
        x_in = [sem(f"x_in{u}") for u in range(4)]
        block = ctx.enter_context(nc.Block())

        x_d = x[0]
        w1_d = w_in[0].rearrange("(k p) (s c) -> p k s c", p=P, c=DM)
        pa_d = nc.dram_tensor("gated_pa", (P, KT, SEQ), f32, kind="Internal").ap()
        x1_d = nc.dram_tensor("x1_saved", (SEQ, DM), f32, kind="Internal").ap()

        CREDIT = 8

        def done(n, j):
            return 4 * n + (CREDIT + j + 1)

        def kept_by(n):
            return n + 2

        def step(S):
            return (0, S // 2) if S % 2 == 0 else (1, TT - 1 - S // 2)

        def step_w(S):
            return P * (step(S)[1] + 1)

        def long_steps(S):
            return sum(step(s)[1] >= 4 for s in range(S))

        PAIRS = [(S, step(S)[0], step(S)[1] // 2) for S in range(2, 2 * TT) if S % 4 >= 2]
        pair_after = {S: q for q, (S, _, _) in enumerate(PAIRS)}

        PASSES = 3 * KT
        gate_upto = [PASSES + -(-PASSES * S // 5) for S in range(2 * TT)]
        gate_ends = {gate_upto.index(PASSES * (j + 1)): j for j in range(4)}

        mix_upto = ([PASSES * (v + 1) // 2 for v in range(8)], [0] + [-(-2 * PASSES * v // 7) for v in range(1, 8)])

        def mix_gate(p, j):
            th, ct = j // 2, j % 2
            if p == 0:
                return OUT[:, ct, th * HALF:(th + 1) * HALF]
            return GV[:, 2 * j:2 * j + 2, 0:BC].rearrange("p a b -> p a b")

        def as_gate(p, ap):
            return ap if p == 0 else ap.rearrange("p (a b) -> p a b", a=2)

        MIX_GROUPS = (slice(4, 8), slice(0, 2), slice(2, 4))

        class FirstNorm:
            def __init__(self, name, eps):
                self.eps = eps
                self.rstd, self.scaled, self.turned = sem(name + "_rstd"), sem(name + "_scaled"), sem(name + "_turned")
                self.hi, self.lo, self.gain = sem(name + "_hi"), sem(name + "_lo"), sem(name + "_gain")

            def act(self, act):
                with act.Fori(0, 2) as i:
                    for u in range(4):
                        act.wait_ge(x_in[u], 16 * i + 16)
                        act.activation(XS[u][:, :], XT[u][:, :], ACT.Square, accum_out=stats[:, u:u + 1])
                        act.drain()
                        act.activation(stats[:, u:u + 1], stats[:, u:u + 1], ACT.Ln, scale=1.0 / DM, bias=self.eps)
                        act.drain()
                        act.activation(stats[:, u:u + 1], stats[:, u:u + 1], ACT.Exp, scale=-0.5).then_inc(self.rstd, 1)
                    for u in range(4):
                        act.wait_ge(self.turned, 4 * i + u + 1)
                        act.activation(A_hi[:, :, ds(512 * i + (META + 128 * u), P)], wide(2 * u).rearrange("p (k c) -> p k c", c=P),
                                       ACT.Copy).then_inc(self.hi, 1)

            def dve(self, dve):
                dve.wait_ge(self.gain, 16)
                with dve.Fori(0, 2) as i:
                    for u in range(4):
                        dve.wait_ge(self.rstd, 4 * i + u + 1)
                        dve.scalar_tensor_tensor(XS[u][:, :], XT[u][:, :], stats[:, u:u + 1], G1[:, :],
                                                 ALU.mult, ALU.mult).then_inc(self.scaled, 1)
                    for u in range(4):
                        dve.wait_ge(self.hi, 4 * i + u + 1)
                        dve.tensor_tensor(A_lo[:, :, ds(512 * i + (META + 128 * u), P)], wide(2 * u).rearrange("p (k c) -> p k c", c=P),
                                          A_hi[:, :, ds(512 * i + (META + 128 * u), P)].bitcast(f32), ALU.subtract).then_inc(self.lo, 1)

            def pe(self, pe):
                with pe.Fori(0, 2) as i:
                    for u in range(4):
                        pe.wait_ge(self.scaled, 4 * i + u + 1)
                        for k in range(KT):
                            last = pe.transpose(wide(2 * u)[:, k * P:(k + 1) * P], XS[u][:, k * P:(k + 1) * P], ident[:, :])
                        last.then_inc(self.turned, 1)

        class LateNorm:
            def __init__(self, name, eps, n, meta_in=None):
                self.eps, self.n, self.meta, self.m = eps, n, meta_in, int(meta_in is not None)
                self.rstd, self.scaled, self.turned = sem(name + "_rstd"), sem(name + "_scaled"), sem(name + "_turned")
                self.hi, self.lo, self.gain = sem(name + "_hi"), sem(name + "_lo"), sem(name + "_gain")

            def parts(self, t):
                if t < 0:
                    return (XT[0][0:META, :], XT[1][0:META, :], stats[0:META, 24:25],
                            bank[4][:, 0:KT * META].rearrange("p (k c) -> p k c", c=META), slice(0, META))
                return (X1[:, t, :], XS[t % 4][:, :], stats[:, 16 + t:17 + t],
                        wide(4 + 2 * (t % 2)).rearrange("p (k c) -> p k c", c=P), slice(META + t * P, META + (t + 1) * P))

            def act_stat(self, act, t):
                src, scr, st, _, _ = self.parts(t)
                if t < 0:
                    act.wait_ge(self.meta, 16)
                else:
                    act.wait_ge(kept[t // 2], kept_by(self.n))
                act.activation(scr, src, ACT.Square, accum_out=st)
                act.drain()
                act.activation(st, st, ACT.Ln, scale=1.0 / DM, bias=self.eps)
                act.drain()
                act.activation(st, st, ACT.Exp, scale=-0.5).then_inc(self.rstd, 1)

            def act_hi(self, act, t):
                _, _, _, turned, c = self.parts(t)
                act.wait_ge(self.turned, self.m + t + 1)
                act.activation(A_hi[:, :, c], turned, ACT.Copy).then_inc(self.hi, 1)

            def act(self, act, next_weights):
                if self.m:
                    self.act_stat(act, -1)
                    self.act_hi(act, -1)
                for j in range(5):
                    if j == 1:
                        next_weights()
                    for t in (2 * j, 2 * j + 1):
                        if j < 4:
                            self.act_stat(act, t)
                    for t in (2 * j - 2, 2 * j - 1):
                        if j:
                            self.act_hi(act, t)

            def dve_scale(self, dve, t):
                src, scr, st, _, _ = self.parts(t)
                dve.wait_ge(self.rstd, self.m + t + 1)
                dve.scalar_tensor_tensor(scr, src, st, G1[0:src.shape[0], :], ALU.mult, ALU.mult).then_inc(self.scaled, 1)

            def dve_lo(self, dve, t):
                _, _, _, turned, c = self.parts(t)
                dve.wait_ge(self.hi, self.m + t + 1)
                dve.tensor_tensor(A_lo[:, :, c], turned, A_hi[:, :, c].bitcast(f32), ALU.subtract).then_inc(self.lo, 1)

            def dve(self, dve, add, next_weights):
                dve.wait_ge(self.gain, 16)
                if self.m:
                    self.dve_scale(dve, -1)
                    self.dve_lo(dve, -1)
                for j in range(5):
                    if j == 1:
                        next_weights()
                    if j < 4:
                        add(j)
                        self.dve_scale(dve, 2 * j)
                        self.dve_scale(dve, 2 * j + 1)
                    if j:
                        self.dve_lo(dve, 2 * j - 2)
                        self.dve_lo(dve, 2 * j - 1)

            def turn(self, pe, t):
                _, scr, _, turned, _ = self.parts(t)
                rows = scr.shape[0]
                pe.wait_ge(self.scaled, self.m + t + 1)
                if self.m + t >= 1 and t != 1:
                    pe.wait_ge(self.lo, self.m + t - (1 if t else 0))
                for k in range(KT):
                    last = pe.transpose(turned[:, k, :], scr[:, k * P:(k + 1) * P], ident[0:rows, 0:rows])
                last.then_inc(self.turned, 1)

            def pe_between(self, pe, j):
                if j:
                    self.turn(pe, 2 * j - 2)
                    self.turn(pe, 2 * j - 1)

        def level_keep(dve, p, v):
            for h in range(2):
                U = 2 * v + h
                dve.wait_ge(lv_done, 16 * p + U + 1)
                if v and h == 0:
                    dve.wait_ge(lv_kept, 16 * p + U)
                for b in range(2):
                    last = dve.copy_predicated(AA[:, 8 * h + 4 * b:8 * h + 4 * b + 4, :],
                                               lvl[:, v, :].bitcast(i32).unsqueeze(1).broadcast_to([P, 4, P]),
                                               bank[2 * (U % 3) + b].rearrange("p (a c) -> p a c", a=4))
                last.then_inc(lv_kept, 1)

        RET_GATE = (6, 7, 4, 5)

        def load_block(sp, n, s, src):
            sp.wait_ge(gp_done, 4 * n + 4)
            w = src.shape[-1]
            sp.dma_start(W_raw[s][:, :, 0:w], src).then_inc(w_loaded[s], 16)

        def split_hi(act, n, s):
            act.wait_ge(w_loaded[s], 8 * n + (16 - 8 * s))
            act.activation(W_hi[s][:, :, :], W_raw[s][:, :, :], ACT.Copy).then_inc(w_hi, 1)

        def split_lo(dve, n, s):
            dve.wait_ge(w_hi, n + 1)
            dve.tensor_tensor(W_lo[s][:, :, :], W_raw[s][:, :, :], W_hi[s][:, :, :].bitcast(f32), ALU.subtract).then_inc(w_lo, 1)

        def gemm(pe, n, s, hi, lo, rows_out, between=None, before=None, banks=range(4)):
            pe.wait_ge(w_lo, n + 1)
            t0 = META if hi is A_hi else 0
            for j in range(4):
                pe.wait_ge(kept[j], n + 1)
                if before:
                    before(j)
                if rows_out:
                    for r in range(2):
                        t = t0 + (2 * j + r) * P
                        for k in range(KT):
                            for g, (a, w) in enumerate(((hi, W_hi), (hi, W_lo), (lo, W_hi))):
                                last = pe.matmul(bank[banks[j]][:, r * BC:(r + 1) * BC], a[:, k, t:t + P], w[s][:, k, :],
                                                 start=(k == 0 and g == 0), stop=(k == KT - 1 and g == 2))
                else:
                    th, ct = j // 2, j % 2
                    for k in range(KT):
                        for g, (w, a) in enumerate(((W_hi, hi), (W_hi, lo), (W_lo, hi))):
                            last = pe.matmul(bank[banks[j]][:, :], w[s][:, k, ct * P:(ct + 1) * P], a[:, k, t0 + th * HALF:t0 + (th + 1) * HALF],
                                             start=(k == 0 and g == 0), stop=(k == KT - 1 and g == 2))
                last.then_inc(gp_done, 1)
                if between:
                    between(j)

        class HeadNorm:
            def __init__(self, name):
                self.sq, self.ss, self.rs = sem(name + "_squared"), sem(name + "_summed"), sem(name + "_rstd")

            def act_square(self, act, src, j):
                act.activation(NB[j][:, :], src, ACT.Square).then_inc(self.sq, 1)

            def act_rstd(self, act, v, j, ss, width, eps):
                act.wait_ge(self.ss, v)
                act.activation(NB[j][:, :], ss, ACT.Ln, scale=1.0 / width, bias=eps)
                act.drain()
                act.activation(NB[j][:, :], NB[j][:, :], ACT.Exp, scale=-0.5).then_inc(self.rs, 1)

        n1 = FirstNorm("norm1", 1e-6)
        hn = HeadNorm("sbnorm")
        z_done, m_ready, l_ready, z_used = sem("z_done"), sem("z_clamped"), sem("softplus_ready"), sem("z_used")
        wgt, tr_done, wt0, wt1 = sem("weights_ready"), sem("turned"), sem("wt_first_kept"), sem("wt_second_kept")
        pv_done, o_kept = sem("pv_done"), sem("attended_kept")
        g_raw, e1 = sem("gate_rows_kept"), sem("sb_gate_ready")
        gated = sem("sb_gated")
        causal_in = sem("causal_in")
        s_hi = [sem(f"branch{b}_hi") for b in range(2)]
        s_lo = [sem(f"branch{b}_lo") for b in range(2)]
        pa_stored = [sem(f"pa_stored{u}") for u in range(2)]
        pa_back = sem("pa_back")
        rtab, dec_in, rot_ok = sem("rotary_tables_in"), sem("decay_in"), sem("rotated")
        a_done, at_ready, rv_part = sem("scores_done"), sem("decayed_ready"), sem("retained_part_done")
        ret_kept = sem("retained_kept")
        rn = HeadNorm("retnorm")
        e3 = sem("ret_gate_ready")
        m_hi, m_lo = sem("merged_hi"), sem("merged_lo")
        xb_in = [sem(f"x_again{u}") for u in range(2)]
        x1_saved, meta_in, swa_in, gla_in = sem("x1_saved"), sem("meta_in"), sem("swa_tables_in"), sem("gla_tables_in")
        L1, B1, L3, B2, L5 = 0, 16, 24, 40, 48
        L6, L7, L8 = 52, 62, 66
        n2 = LateNorm("norm2", 1e-5, L6 - 1, meta_in)
        n3 = LateNorm("norm3", 1e-5, L8 - 1)
        q_raw, q_rot, skr_ok, dup_done, sk_ok = sem("rope_raw"), sem("rope_rotated"), sem("keys_roped"), sem("keys_doubled"), sem("keys_kept")
        km_ok, km_turned, km_raw, v_turned = sem("meta_keys_kept"), sem("meta_keys_turned"), sem("meta_keys_raw"), sem("values_turned")
        sv_zero, sv_ok, extra, extra_kept = sem("sv_zeroed"), sem("sv_kept"), sem("meta_product_done"), sem("meta_product_kept")
        s_done, s_copied, s_max, s_exp, p_ready = sem("swa_scores"), sem("swa_copied"), sem("swa_max"), sem("swa_exp"), sem("swa_probs")
        t_done, pt_a, pt_d, so_done, so_kept = sem("swa_turned"), sem("pt_by_act"), sem("pt_by_dve"), sem("swa_out"), sem("swa_out_kept")
        lr_ok, gx_done, gx_clamped, gx_l, gx_r, gb_ok = sem("lr_kept"), sem("gate_product"), sem("gate_clamped"), sem("gate_ln"), sem("gate_relu"), sem("decay_ok")
        ge_sub, ge_exp, qk_ok, lv_done, lv_kept = sem("ref_sub"), sem("ref_exp"), sem("level_operands_ok"), sem("level_done"), sem("level_kept")
        kt_done, kt_ok, u_done, st_ok, go_done, go_kept = sem("k_turned"), sem("k_turned_kept"), sem("update_done"), sem("state_ok"), sem("gla_out"), sem("gla_out_kept")
        gn = HeadNorm("glanorm")
        aa_zero = sem("scores_zeroed")
        mg_raw, mg_ok = sem("mix_gate_kept"), sem("mix_gate_ready")
        qe_ok2 = sem("state_operands_ok")
        f_relu, f_hi = sem("relu_ready"), sem("hidden_hi")
        c_hi, c_lo = sem("mix_hi"), sem("mix_lo")
        x1_in = [sem(f"x1_again{u}") for u in range(2)]
        fin_rstd, fin_ok, fin_gain = sem("final_rstd"), sem("final_ok"), sem("final_gain")
        y_out = [sem(f"y_stored{u}") for u in range(4)]

        COLS = {}
        spec = [("q_gain", sb_q_gain[0].rearrange("(r c) -> r c", c=P)), ("k_gain", sb_k_gain[0].rearrange("(r c) -> r c", c=P)),
                ("ret_gain", ret_out_gain[0].rearrange("h (r c) -> (h r) c", c=P)),
                ("merge", b_merge[0].rearrange("b (r c) -> (b r) c", c=P)),
                ("gate_b", b_gate_2[0].rearrange("(r c) -> r c", c=P)), ("gla_gain", gla_norm_w_2[0].rearrange("(r c) -> r c", c=P))]
        r0 = 0
        for name, a in spec:
            COLS[name] = r0
            r0 += a.shape[0]
        NROWS = r0

        @block.sync
        def _(sp):
            sp.dma_start(ident[:, :], tab["ident"]).then_inc(const_in, 16)
            for name, a in spec:
                sp.dma_start(rows[COLS[name]:COLS[name] + a.shape[0], :], a).then_inc(const_in, 16)
            for t in range(4):
                sp.dma_start(XT[t][:, :], x_d[t * P:(t + 1) * P, :]).then_inc(x_in[t], 16)
            sp.dma_start(G1[:, :], norm_gain[0, :].partition_broadcast(P)).then_inc(n1.gain, 16)
            for s in range(2):
                load_block(sp, L1 + s, s, w1_d[:, :, s, 0:BC])
            for t in range(4, 8):
                sp.wait_ge(n1.scaled, t - 3)
                sp.dma_start(XT[t - 4][:, :], x_d[t * P:(t + 1) * P, :]).then_inc(x_in[t - 4], 16)
            for s in range(2, 4):
                load_block(sp, L1 + s, s % 2, w1_d[:, :, s, 0:BC])
            with sp.Fori(1, 4) as i:
                for s in range(4):
                    load_block(sp, L1 + 4 * i + s, s % 2, w1_d[:, :, s, ds(i * BC, BC)])
            for b, (B, Lb, sec, wb) in enumerate(((B1, L3, 8, w_branch_sb), (B2, L5, 9, w_branch_ret))):
                wb_d = wb[0].rearrange("(k p) c -> p k c", p=P)
                load_block(sp, B, 0, w1_d[:, :, sec, 0:BC])
                load_block(sp, B + 1, 1, wb_d[:, :, 0:BC])
                with sp.Fori(0, 3) as i:
                    load_block(sp, B + 2 * i + 2, 0, w1_d[:, :, sec, ds(i * BC + BC, BC)])
                    load_block(sp, B + 2 * i + 3, 1, wb_d[:, :, ds(i * BC + BC, BC)])
                if b == 0:
                    with sp.Fori(0, 4) as i:
                        for s in range(4):
                            load_block(sp, L3 + 4 * i + s, s % 2, w1_d[:, :, 4 + s, ds(i * BC, BC)])
            wo_d = w_out[0].rearrange("(k p) c -> p k c", p=P)
            with sp.Fori(0, 2) as i:
                for s in range(2):
                    load_block(sp, L5 + 2 * i + s, s, wo_d[:, :, ds(i * (2 * BC) + s * BC, BC)])
            w6_d = w_in_2[0].rearrange("(k p) c -> p k c", p=P)
            for m, c in enumerate((1552, 1808, 2064, 0, 256, 1536, 512, 768, 1024, 1280)):
                load_block(sp, L6 + m, m % 2, w6_d[:, :, c:c + BC])
            w7_d = w_out_2[0].rearrange("(k p) c -> p k c", p=P)
            with sp.Fori(0, 2) as i:
                for s in range(2):
                    load_block(sp, L7 + 2 * i + s, s, w7_d[:, :, ds(i * (2 * BC) + s * BC, BC)])
            f1_d = w_ff1_2[0].rearrange("(k p) c -> p k c", p=P)
            f2_d = w_ff2_2[0].rearrange("(g k p) c -> p g k c", p=P, k=KT)
            with sp.Fori(0, 4) as i:
                for s in range(4):
                    load_block(sp, L8 + 8 * i + s, s % 2, f1_d[:, :, ds(i * (4 * BC) + s * BC, BC)])
                for s in range(4):
                    load_block(sp, L8 + 8 * i + 4 + s, s % 2, f2_d[:, ds(i, 1), :, s * BC:(s + 1) * BC].rearrange("p g k c -> p (g k) c"))
            sp.wait_ge(gp_done, done(L8 + 27, 3))
            sp.dma_start(GF[:, :], final_norm_w_2[:].partition_broadcast(P)).then_inc(fin_gain, 16)
            for t in range(TT):
                sp.wait_ge(fin_ok, t + 1)
                sp.dma_start(out[0, t * P:(t + 1) * P, :], YB[t % 4][:, :]).then_inc(y_out[t % 4], 16)
            for u in range(4):
                sp.wait_ge(y_out[u], 32)

        @block.gpsimd
        def _(pool):
            pool.memset(ones[:, :], 1.0).then_inc(const_ok, 1)
            pool.wait_ge(n1.lo, 8)
            pool.dma_start(causal[:, :], tab["causal"]).then_inc(causal_in, 16)
            with pool.Fori(0, 4) as i:
                for j in range(4):
                    th, ct = j // 2, j % 2
                    pool.wait_ge(kept[j], kept_by(B1 + 2 * i + 1))
                    pool.dma_start(pa_d[:, ds(2 * i + ct, 1), th * HALF:(th + 1) * HALF].rearrange("p a b -> p (a b)"),
                                   stage[j % 2][:, :]).then_inc(pa_stored[j % 2], 16)
            for u in range(2):
                pool.wait_ge(pa_stored[u], 16 * 8)
            pool.wait_ge(gp_done, done(B1 + 7, 3))
            pool.dma_start(rcos[:, :], tab["rcos"]).then_inc(rtab, 16)
            pool.dma_start(rsin[:, :], tab["rsin"]).then_inc(rtab, 16)
            pool.dma_start(decay[:, :], tab["decay"][0]).then_inc(dec_in, 16)
            with pool.Fori(1, 4) as i:
                pool.wait_ge(at_ready, 8 * i)
                pool.dma_start(decay[:, :], tab["decay"][ds(i, 1)].rearrange("a p c -> (a p) c")).then_inc(dec_in, 16)
            pool.wait_ge(s_lo[1], KT)
            pool.dma_start(OUT[:, :, :], pa_d).then_inc(pa_back, 16)
            pool.wait_ge(gp_done, done(B2 + 7, 3))
            pool.dma_start(G1[:, :], norm_mix_w_2[0, :].partition_broadcast(P)).then_inc(n2.gain, 16)
            pool.dma_start(XT[0][0:META, :], meta_tokens_2).then_inc(meta_in, 16)
            for dst, src in ((pcos[:, :], tab["pcos"]), (psin[:, :], tab["psin"]), (rot[:, :], tab["rot"]),
                             (dup[:, :, :], tab["dup"].rearrange("g p c -> p g c")), (window[:, :], tab["window"]),
                             (sinks[:, :], sinks_2[0, :].partition_broadcast(P))):
                pool.dma_start(dst, src).then_inc(swa_in, 16)
            with pool.Fori(0, 2) as i:
                for s in range(2):
                    n = L5 + 2 * i + s
                    for j in range(4):
                        pool.wait_ge(kept[(j + 2) % 4], n + 1 + j // 2)
                        pool.dma_start(XB[j % 2][:, :, :], x_d[2 * j * P:(2 * j + 2) * P, ds(i * (2 * BC) + s * BC, BC)]
                                       .rearrange("(a p) c -> p a c", p=P)).then_inc(xb_in[j % 2], 16)
            for j in range(4):
                pool.wait_ge(kept[j], kept_by(L5 + 3))
            pool.dma_start(x1_d.rearrange("(t p) d -> p t d", p=P), X1[:, :, :]).then_inc(x1_saved, 16)
            pool.wait_ge(n2.lo, TT + 1)
            pool.memset(SV[:, :, :, :], 0.0).then_inc(sv_zero, 1)
            pool.memset(SVM[:, :, :], 0.0).then_inc(sv_zero, 1)
            pool.wait_ge(so_kept, 16)
            for dst, src in ((wgu[:, :], w_gate_up_2[0]), (lvl[:, :, :], tab["levels"]), (restart[:, :], tab["restart"])):
                pool.dma_start(dst, src).then_inc(gla_in, 16)
            pool.memset(AA[:, :, :], 0.0).then_inc(aa_zero, 1)
            pool.wait_ge(go_done, TT)
            pool.memset(AA[:, :, :], 0.0).then_inc(aa_zero, 1)
            pool.wait_ge(go_kept, 8)
            pool.dma_start(G1[:, :], norm_ff_w_2[0, :].partition_broadcast(P)).then_inc(n3.gain, 16)
            with pool.Fori(0, 2) as i:
                for s in range(2):
                    n = L7 + 2 * i + s
                    for j in range(4):
                        pool.wait_ge(kept[(j + 2) % 4], n + 1 + j // 2)
                        pool.dma_start(XB[j % 2][:, :, :], x1_d[2 * j * P:(2 * j + 2) * P, ds(i * (2 * BC) + s * BC, BC)]
                                       .rearrange("(a p) c -> p a c", p=P)).then_inc(x1_in[j % 2], 16)

        @block.scalar
        def _(act):
            act.preload_act_table_set(LOG_EXP)
            n1.act(act)

            def plain_keep(n, j, dst):
                act.wait_ge(gp_done, done(n, j))
                act.activation(dst, bank[j], ACT.Copy).then_inc(kept[j], 1)

            def gates(n, e, func, table, bias=lambda j: 0.0, outputs=range(4), banks=range(4)):
                act.preload_act_table_set(table)
                for j in outputs:
                    act.wait_ge(gp_done, done(n, j))
                    act.activation(NB[j][:, :], bank[banks[j]], func, bias=bias(j)).then_inc(e if e else kept[j], 1)
                act.preload_act_table_set(LOG_EXP)

            split_hi(act, L1, 0)
            with act.Fori(0, 4) as i:
                n = L1 + 4 * i
                for m in range(9):
                    if m % 4 == 0:
                        split_hi(act, n + m // 4 + 1, (m // 4 + 1) % 2)
                    if m < 8:
                        act.wait_ge(gp_done, done(n + m // 4, m % 4))
                        if m < 4:
                            act.wait_ge(gated, 4 * i + m + 1)
                        hn.act_square(act, bank[m % 4], m % 4)
                    else:
                        plain_keep(n + 2, 0, V[:, 0:2, :].rearrange("p a b -> p (a b)"))
                    if m >= 1:
                        hn.act_rstd(act, 8 * i + m, (m - 1) % 4, bank[4 + (m - 1) % 2], 128, 1e-6)
                for j in range(1, 4):
                    plain_keep(n + 2, j, V[:, 2 * j:2 * j + 2, :].rearrange("p a b -> p (a b)"))

                def softplus_terms(S, between=None):
                    w = step_w(S)
                    act.wait_ge(m_ready, 16 * i + S + 1)
                    act.activation(L[S % 2][:, 0:w], L[S % 2][:, 0:w], ACT.Exp)
                    act.activation(R[S % 2][:, 0:w], wide(4 + 2 * (S % 2), w), ACT.Relu, bias=-CLAMP)
                    if between is not None:
                        keep_first(between)
                    act.drain()
                    act.activation(L[S % 2][:, 0:w], L[S % 2][:, 0:w], ACT.Ln, bias=1.0).then_inc(l_ready, 1)

                def keep_first(S):
                    c, qt = step(S)
                    nb = min(qt + 1, 4)
                    act.wait_ge(tr_done, 16 * i + S + 1)
                    act.activation(WT[c][:, 0:nb, (qt % 2) * P:(qt % 2 + 1) * P], bank[0][:, 0:nb * P].rearrange("p (a b) -> p a b", b=P),
                                   ACT.Copy).then_inc(wt0, 1)

                def keep_gate(j):
                    act.wait_ge(gp_done, done(n + 3, j))
                    act.activation(NB[j][:, :], bank[3], ACT.Copy).then_inc(g_raw, 1)

                softplus_terms(0)
                softplus_terms(1)
                for S in range(16):
                    w = step_w(S)
                    act.wait_ge(z_used, 16 * i + S + 1)
                    act.activation(C[S % 2][:, 0:w], C[S % 2][:, 0:w], ACT.Exp).then_inc(wgt, 1)
                    if S - 1 in gate_ends:
                        keep_gate(gate_ends[S - 1])
                    if S < 14:
                        softplus_terms(S + 2, S)
                    else:
                        keep_first(S)
                    if S == 7:
                        split_hi(act, n + 4, 0)
                keep_gate(3)
                act.drain()
                act.preload_act_table_set("silu_and_others")
                for j in range(4):
                    act.activation(NB[j][:, :], NB[j][:, :], ACT.Silu).then_inc(e1, 1)
                act.preload_act_table_set(LOG_EXP)

            def branch(b, B):
                if b == 0:
                    act.wait_ge(gated, 4 * 4 + 4)
                for j in range(4):
                    act.wait_ge(kept[j], kept_by(B - 1))
                for k in range(KT):
                    act.activation(S_hi[:, k, :], OUT[:, k, :], ACT.Copy).then_inc(s_hi[b], 1)
                with act.Fori(0, 4) as i:
                    n = B + 2 * i
                    split_hi(act, n + 1, 1)
                    act.drain()
                    act.activation(stats[:, 8:10], cols[:, ds(2 * i + (COLS["merge"] + 8 * b), 2)], ACT.Copy)
                    act.drain()
                    gates(n, None, ACT.Sigmoid, "sigmoid_and_others", bias=lambda j: stats[:, 8 + j % 2:9 + j % 2])
                    split_hi(act, n + 2, 0)

            branch(0, B1)
            with act.Fori(0, 4) as i:
                n = L3 + 4 * i
                split_hi(act, n + 1, 1)
                split_hi(act, n + 2, 0)
                split_hi(act, n + 3, 1)
                for j in range(4):
                    plain_keep(n + 2, j, RV[:, 2 * j:2 * j + 2, :].rearrange("p a b -> p (a b)"))
                act.wait_ge(rv_part, 8 * i + 8)
                for j in range(4):
                    rn.act_square(act, bank[j], j)
                for th in range(2):
                    rn.act_rstd(act, 2 * i + th + 1, 2 * th, bank[4 + th], 256, 1e-6)
                act.wait_ge(ret_kept, 4 * i + 4)
                split_hi(act, n + 4, 0)
                gates(n + 3, e3, ACT.Silu, "silu_and_others", banks=RET_GATE)
            branch(1, B2)
            act.wait_ge(gp_done, done(B2 + 6, 3))
            for j in range(4):
                act.wait_ge(kept[j], kept_by(B2 + 5))
            for k in range(6):
                act.activation(A_hi[:, k, META:NT], OUT[:, k, :], ACT.Copy).then_inc(m_hi, 1)
            for j in range(4):
                th, ct = j // 2, j % 2
                act.wait_ge(kept[j], kept_by(B2 + 7))
                act.activation(A_hi[:, 6 + ct, META + th * HALF:META + (th + 1) * HALF], OUT[:, 6 + ct, th * HALF:(th + 1) * HALF],
                               ACT.Copy).then_inc(m_hi, 1)
            for b in range(1, 4):
                split_hi(act, L5 + b, b % 2)
            n2.act(act, lambda: split_hi(act, L6, 0))

            act.wait_ge(sv_zero, 2)
            for b in range(2):
                n = L6 + b
                split_hi(act, n + 1, (b + 1) % 2)
                for j in range(4):
                    act.wait_ge(gp_done, done(n, j))
                    act.activation(NB[j][:, :], bank[j], ACT.Copy, scale=0.125).then_inc(q_raw, 1)
            n = L6 + 2
            split_hi(act, n + 1, 1)
            act.wait_ge(extra, 1)
            act.activation(SVM[:, :, 64:128], bank[7][0:META, P:BC].rearrange("p (g d) -> p g d", g=2), ACT.Copy).then_inc(sv_ok, 1)
            act.activation(KMT[:, :], bank[7][0:META, 0:P], ACT.Copy).then_inc(km_ok, 1)
            for j in range(4):
                act.wait_ge(gp_done, done(n, j))
                act.activation(NB[j][:, :], bank[j], ACT.Copy).then_inc(kept[j] if j % 2 else q_raw, 1)
                if j == 1:
                    act.wait_ge(km_turned, 1)
                    act.activation(KMR[:, :], bank[7][:, 0:META], ACT.Copy).then_inc(km_raw, 1)
            for h in range(2):
                act.wait_ge(v_turned, h + 1)
                act.activation(SV[:, 4 * h:4 * h + 4, :, 64:128], bank[6 + h].rearrange("p (t g d) -> p t g d", t=4, g=2), ACT.Copy).then_inc(sv_ok, 1)
            for g in range(2):
                for c, (lo, hi) in enumerate(((META, META + HALF), (META + HALF, NT), (0, META))):
                    act.wait_ge(dup_done, 3 * g + c + 1)
                    act.activation(SK[:, g, lo:hi], bank[(3 * g + c) % 4][:, 0:hi - lo], ACT.Copy).then_inc(sk_ok, 1)

            def window_exp(E):
                lo = P if E < 2 else 0
                act.wait_ge(s_max, E + 1)
                for h in range(4):
                    act.activation(SS[E % 3][:, h, lo:], SS[E % 3][:, h, lo:], ACT.Exp, bias=SM[:, E % 3, 0, h:h + 1],
                                   accum_out=SM[:, E % 3, 1, h:h + 1])
                act.activation(SM[:, E % 3, 2, :], SM[:, E % 3, 2, :], ACT.Exp).then_inc(s_exp, 1)

            window_exp(0)
            window_exp(1)
            for E in range(16):
                if E < 14:
                    window_exp(E + 2)
                act.wait_ge(t_done, E + 1)
                if E >= 2:
                    act.activation(PT[E % 2][0][:, :], bank[4], ACT.Copy)
                act.activation(PT[E % 2][2][0:META, :], bank[6][0:META, :], ACT.Copy).then_inc(pt_a, 1)

            act.wait_ge(so_kept, 16)
            split_hi(act, L6 + 4, 0)
            for j in range(4):
                th, ct = j // 2, j % 2
                act.wait_ge(gp_done, done(L6 + 3, j))
                act.activation(GQ[:, ct, th * HALF:(th + 1) * HALF], bank[j], ACT.Copy, scale=0.125).then_inc(kept[j], 1)
            split_hi(act, L6 + 5, 1)
            for j in range(4):
                th, ct = j // 2, j % 2
                plain_keep(L6 + 4, j, GK[:, ct, META + th * HALF:META + (th + 1) * HALF])
            act.wait_ge(extra, 2)
            act.activation(GK[:, :, 0:META], bank[6][:, 0:2 * META].rearrange("p (c t) -> p c t", c=2), ACT.Copy).then_inc(extra_kept, 1)
            split_hi(act, L6 + 6, 0)
            for j in range(2):
                act.wait_ge(gp_done, done(L6 + 5, j))
                act.activation(LR[:, META + j * HALF:META + (j + 1) * HALF], bank[j][0:16, :], ACT.Copy).then_inc(kept[j], 1)
            act.wait_ge(extra, 3)
            act.activation(LR[:, 0:META], bank[6][0:16, 0:META], ACT.Copy).then_inc(lr_ok, 1)
            pieces = [(c, lo, hi) for c in range(2) for lo, hi in ((META, META + HALF), (META + HALF, NT), (0, META))]
            for m, (c, lo, hi) in enumerate(pieces):
                w = hi - lo
                act.wait_ge(gx_clamped, m + 1)
                act.activation(GT[m % 2][:, 0:w], bank[4 + m % 2][:, 0:w], ACT.Relu, scale=-1.0, bias=GD[:, c:c + 1])
                act.activation(GB[:, c, lo:hi], GB[:, c, lo:hi], ACT.Exp, scale=-1.0)
                act.drain()
                act.activation(GB[:, c, lo:hi], GB[:, c, lo:hi], ACT.Ln, bias=1.0).then_inc(gx_l, 1)

            def level_exp(p, v):
                act.wait_ge(ge_sub, 9 * p + v + 1)
                act.activation(GE[:, :], GE[:, :], ACT.Abs)
                act.drain()
                act.activation(GE[:, :], GE[:, :], ACT.Exp, scale=-1.0 / 16).then_inc(ge_exp, 1)

            level_exp(0, 0)
            for b in range(2):
                n = L6 + 6 + b
                split_hi(act, n + 1, (b + 1) % 2)
                for j in range(4):
                    plain_keep(n, j, GV[:, 2 * j:2 * j + 2, b * BC:(b + 1) * BC])
                act.wait_ge(extra, 4 + b)
                act.activation(GVM[:, b * BC:(b + 1) * BC], bank[7][0:META, 0:BC], ACT.Copy).then_inc(extra_kept, 1)

            NL = len(GLA_LEVELS)

            def keep_mix_gate(p, j):
                act.wait_ge(gp_done, done(L6 + 8 + p, j))
                act.activation(mix_gate(p, j), as_gate(p, bank[0 + j % 2 if p and j >= 2 else 6 + j % 2]), ACT.Copy).then_inc(mg_raw, 1)

            def mix_gates_after(p, v):
                for j in range(4):
                    if (mix_upto[p][v - 1] if v else 0) < PASSES * (j + 1) <= mix_upto[p][v]:
                        keep_mix_gate(p, j)

            def silu_mix_gates(g):
                act.drain()
                act.activation(g, g, ACT.Silu).then_inc(mg_ok, 1)

            def mix_hi(th, g):
                k = MIX_GROUPS[g]
                act.activation(A_hi[:, k, META + th * HALF:META + (th + 1) * HALF], OUT[:, k, th * HALF:(th + 1) * HALF],
                               ACT.Copy).then_inc(c_hi, 1)

            for p in range(2):
                for v in range(1, NL - 1):
                    level_exp(p, v)
                    if p == 0 or v >= 2:
                        mix_gates_after(p, v - 1)
                    if v == 4:
                        split_hi(act, L6 + 9 + p, (p + 1) % 2)
                act.wait_ge(ge_sub, 9 * p + NL)
                act.activation(GE[:, :], GB[:, p, META:NT], ACT.Exp, scale=-1.0 / 16)
                act.activation(GD[:, 2:2 + TT], GB[:, p, META + P - 1:NT:P], ACT.Exp, scale=-1.0 / 16).then_inc(ge_exp, 1)
                act.wait_ge(ge_sub, 9 * p + NL + 1)
                act.activation(KEM[:, :], KEM[:, :], ACT.Exp, scale=1.0 / 16)
                act.activation(GE[:, :], GE[:, :], ACT.Exp, scale=1.0 / 16).then_inc(ge_exp, 1)
                mix_gates_after(p, NL - 2)
                mix_gates_after(p, NL - 1)
                act.wait_ge(kt_done, p + 1)
                act.activation(KTK[:, :, :], wide(6).rearrange("p (t c) -> p t c", c=P), ACT.Copy)
                act.activation(KTM[:, :], bank[2][0:META, 0:P], ACT.Copy).then_inc(kt_ok, 1)
                if p == 0:
                    level_exp(1, 0)
                    act.preload_act_table_set("silu_and_others")
                    silu_mix_gates(OUT[:, 0:2, :])
                    act.preload_act_table_set(LOG_EXP)
                else:
                    mix_hi(0, 0)
                    mix_hi(0, 1)
                act.wait_ge(go_done, TT * p + TT)
                for j in range(4):
                    gn.act_square(act, bank[4 + j], j)
                if p:
                    keep_mix_gate(1, 2)
                for j in range(4):
                    gn.act_rstd(act, 4 * p + j + 1, j, bank[2 + j % 2], 128, 1e-5)
            act.preload_act_table_set("silu_and_others")
            silu_mix_gates(GV[:, 0:4, 0:BC])
            act.wait_ge(go_kept, 6)
            mix_hi(0, 2)
            keep_mix_gate(1, 3)
            silu_mix_gates(GV[:, 4:8, 0:BC])
            mix_hi(1, 0)
            mix_hi(1, 1)
            act.wait_ge(go_kept, 8)
            mix_hi(1, 2)
            act.preload_act_table_set(LOG_EXP)
            for b in range(1, 4):
                split_hi(act, L7 + b, b % 2)
            n3.act(act, lambda: split_hi(act, L8, 0))

            def ff_turn(i, last):
                n = L8 + 8 * i
                for b in range(4):
                    split_hi(act, n + b + 1, (b + 1) % 2)
                    for j in range(4):
                        th, ct = j // 2, j % 2
                        act.wait_ge(gp_done, done(n + b, j))
                        act.activation(NB[j][:, :], bank[j], ACT.Relu)
                        act.drain()
                        act.activation(F_hi[:, 2 * b + ct, th * HALF:(th + 1) * HALF], NB[j][:, :], ACT.Square).then_inc(f_hi, 1)
                for b in range(4):
                    if not last or b < 3:
                        split_hi(act, n + 4 + b + 1, (b + 1) % 2)
            with act.Fori(0, 3) as i:
                ff_turn(i, False)
            ff_turn(3, True)
            for t in range(TT):
                u = t % 4
                act.wait_ge(kept[t // 2], kept_by(L8 + 31))
                if t >= 4:
                    act.wait_ge(y_out[u], 16)
                act.activation(YB[u][:, :], X1[:, t, :], ACT.Square, accum_out=stats[:, t:t + 1])
                act.drain()
                act.activation(stats[:, t:t + 1], stats[:, t:t + 1], ACT.Ln, scale=1.0 / DM, bias=1e-5)
                act.drain()
                act.activation(stats[:, t:t + 1], stats[:, t:t + 1], ACT.Exp, scale=-0.5).then_inc(fin_rstd, 1)

        @block.vector
        def _(dve):
            for j in range(4):
                dve.sem_inc(kept[j], 1)
            dve.sem_inc(gated, 4)
            dve.wait_ge(const_ok, 2)
            dve.tensor_copy(cols[:, 0:NROWS], bank[7][:, 0:NROWS])
            dve.drain()
            g = COLS["q_gain"]
            dve.tensor_scalar(cols[:, g:g + 1], cols[:, g:g + 1], P ** -0.5, None, ALU.mult).then_inc(const_ok, 1)
            n1.dve(dve)

            def silu_gate(n, i, e, outputs=range(4)):
                for j in outputs:
                    th, ct = j // 2, j % 2
                    dst = OUT[:, ds(2 * i + ct, 1), th * HALF:(th + 1) * HALF].rearrange("p a b -> p (a b)")
                    dve.wait_ge(e, 4 * i + j + 1)
                    dve.tensor_tensor(dst, dst, NB[j][:, :], ALU.mult).then_inc(gated if e is e1 else kept[j], 1)

            split_lo(dve, L1, 0)
            with dve.Fori(0, 4) as i:
                n = L1 + 4 * i
                for m in range(8):
                    if m % 4 == 0:
                        split_lo(dve, n + m // 4 + 1, (m // 4 + 1) % 2)
                    j = m % 4
                    th, ct = j // 2, j % 2
                    dve.wait_ge(hn.rs, 8 * i + m + 1)
                    g = COLS["q_gain"] if m < 4 else COLS["k_gain"]
                    dve.scalar_tensor_tensor((Q if m < 4 else K)[:, ct, th * HALF:(th + 1) * HALF], bank[j], cols[:, g:g + 1],
                                             NB[j][:, :], ALU.mult, ALU.mult).then_inc(kept[j], 1)
                split_lo(dve, n + 3, 1)

                def clamp(S):
                    w = step_w(S)
                    dve.wait_ge(z_done, 16 * i + S + 1)
                    dve.tensor_scalar(L[S % 2][:, 0:w], wide(4 + 2 * (S % 2), w), CLAMP, None, ALU.min).then_inc(m_ready, 1)

                def keep_second(S):
                    c, qt = step(S)
                    nb = qt + 1 - 4
                    if nb > 0:
                        dve.wait_ge(tr_done, 16 * i + S + 1)
                        dve.tensor_copy(WT[c][:, 4:4 + nb, (qt % 2) * P:(qt % 2 + 1) * P],
                                        bank[1][:, 0:nb * P].rearrange("p (a b) -> p a b", b=P)).then_inc(wt1, 1)

                def keep_attended(q):
                    dve.wait_ge(pv_done, 8 * i + q + 1)
                    _, c, m = PAIRS[q]
                    dve.tensor_copy(OUT[:, ds(2 * i + c, 1), m * 2 * P:(m + 1) * 2 * P].rearrange("p a b -> p (a b)"),
                                    bank[2][:, 0:2 * P]).then_inc(o_kept, 1)

                def suffix_sum(S):
                    w = step_w(S)
                    dve.wait_ge(l_ready, 16 * i + S + 1)
                    if S >= 2:
                        dve.wait_ge(tr_done, 16 * i + S - 1)
                    dve.tensor_tensor_scan(C[S % 2][:, 0:w][:, ::-1], L[S % 2][:, 0:w][:, ::-1], R[S % 2][:, 0:w][:, ::-1], 0.0, ALU.add, ALU.add)

                clamp(0)
                clamp(1)
                suffix_sum(0)
                for S in range(16):
                    w = step_w(S)
                    if S - 2 in pair_after:
                        keep_attended(pair_after[S - 2])
                    dve.drain()
                    dve.tensor_tensor(C[S % 2][:, 0:w], wide(4 + 2 * (S % 2), w), C[S % 2][:, 0:w], ALU.subtract).then_inc(z_used, 1)
                    if S >= 1:
                        keep_second(S - 1)
                    if S < 15:
                        suffix_sum(S + 1)
                    if S < 14:
                        clamp(S + 2)
                    if S == 8:
                        split_lo(dve, n + 4, 0)
                keep_attended(6)
                keep_second(15)
                keep_attended(7)
                dve.drain()
                for j in range(4):
                    dve.sem_inc(kept[j], 1)
                silu_gate(n + 3, i, e1)

            def branch(b, B):
                for k in range(KT):
                    dve.wait_ge(s_hi[b], k + 1)
                    dve.tensor_tensor(S_lo[:, k, :], OUT[:, k, :], S_hi[:, k, :].bitcast(f32), ALU.subtract).then_inc(s_lo[b], 1)

                def turn(i, first, last=False):
                    n = B + 2 * i
                    split_lo(dve, n + 1, 1)
                    split_lo(dve, n + 2, 0)
                    if b and first:
                        dve.wait_ge(pa_back, 16)
                    if last:
                        for k in range(6):
                            merged_lo(k + 1, k, slice(0, SEQ))
                    for j in range(4):
                        th, ct = j // 2, j % 2
                        dve.wait_ge(gp_done, done(n + 1, j))
                        dve.wait_ge(kept[j], kept_by(n))
                        if b == 0:
                            if not first or j >= 2:
                                dve.wait_ge(pa_stored[j % 2], 32 * i + 16 * (j // 2))
                            dve.tensor_tensor(stage[j % 2][:, :], bank[j], NB[j][:, :], ALU.mult).then_inc(kept[j], 1)
                        else:
                            dst = OUT[:, ds(2 * i + ct, 1), th * HALF:(th + 1) * HALF].rearrange("p a b -> p (a b)")
                            dve.tensor_tensor(NB[j][:, :], bank[j], NB[j][:, :], ALU.mult)
                            dve.drain()
                            dve.tensor_tensor(dst, dst, NB[j][:, :], ALU.add).then_inc(kept[j], 1)
                            if last and j % 2:
                                for c in range(2):
                                    merged_lo(7 + 2 * th + c, 6 + c, slice(th * HALF, (th + 1) * HALF))

                def merged_lo(v, k, t):
                    dve.wait_ge(m_hi, v)
                    dve.tensor_tensor(A_lo[:, k, META + t.start:META + t.stop], OUT[:, k, t],
                                      A_hi[:, k, META + t.start:META + t.stop].bitcast(f32), ALU.subtract).then_inc(m_lo, 1)

                turn(0, True)
                with dve.Fori(1, 4 - b) as i:
                    turn(i, False)
                if b:
                    turn(3, False, True)

            branch(0, B1)
            dve.wait_ge(rtab, 32)
            with dve.Fori(0, 4) as i:
                n = L3 + 4 * i
                for b, dst in enumerate((RQ, RK)):
                    split_lo(dve, n + b + 1, (b + 1) % 2)
                    for th in range(2):
                        c, s = rcos[:, th * HALF:(th + 1) * HALF], rsin[:, th * HALF:(th + 1) * HALF]
                        t1, t2 = bank[2 * th], bank[2 * th + 1]
                        dve.wait_ge(gp_done, done(n + b, 2 * th + 1))
                        dve.tensor_tensor(RT[0][:, :], t1, c, ALU.mult)
                        dve.tensor_tensor(RT[1][:, :], t2, s, ALU.mult)
                        dve.tensor_tensor(RT[2][:, :], t1, s, ALU.mult).then_inc(kept[2 * th], 1)
                        dve.tensor_tensor(RT[3][:, :], t2, c, ALU.mult).then_inc(kept[2 * th + 1], 1)
                        dve.drain()
                        dve.tensor_tensor(dst[:, 0, th * HALF:(th + 1) * HALF], RT[0][:, :], RT[1][:, :], ALU.subtract)
                        dve.tensor_tensor(dst[:, 1, th * HALF:(th + 1) * HALF], RT[2][:, :], RT[3][:, :], ALU.add).then_inc(rot_ok, 1)
                        dve.drain()
                split_lo(dve, n + 3, 1)
                dve.wait_ge(dec_in, 16 * i + 16)
                for kb in range(TT):
                    w = SEQ - P * kb
                    dve.wait_ge(a_done, 8 * i + kb + 1)
                    if kb >= 2:
                        dve.wait_ge(rv_part, 8 * i + kb - 1)
                    dve.tensor_tensor(AT[kb % 2][:, 0:w], wide(4 + 2 * (kb % 2), w), decay[:, 0:w], ALU.mult).then_inc(at_ready, 1)
                for j in range(4):
                    th, ct = j // 2, j % 2
                    dve.wait_ge(rn.rs, 2 * i + th + 1)
                    dve.scalar_tensor_tensor(OUT[:, ds(2 * i + ct, 1), th * HALF:(th + 1) * HALF].rearrange("p a b -> p (a b)"), bank[j],
                                             cols[:, ds(2 * i + (COLS["ret_gain"] + ct), 1)], NB[2 * th][:, :],
                                             ALU.mult, ALU.mult).then_inc(ret_kept, 1)
                dve.drain()
                split_lo(dve, n + 4, 0)
                silu_gate(n + 3, i, e3)
            branch(1, B2)

            def residual_blocks(B, again, norm):
                def add(b, j):
                    dve.wait_ge(gp_done, done(B + b, j))
                    dve.wait_ge(again[j % 2], 32 * b + 16 * (j // 2) + 16)
                    dve.tensor_tensor(X1[:, 2 * j:2 * j + 2, b * BC:(b + 1) * BC], bank[j].rearrange("p (a c) -> p a c", a=2),
                                      XB[j % 2][:, :, :], ALU.add).then_inc(kept[j], 1)
                for b in range(3):
                    split_lo(dve, B + b + 1, (b + 1) % 2)
                    for j in range(4):
                        add(b, j)
                norm.dve(dve, lambda j: add(3, j), lambda: split_lo(dve, B + 4, 0))

            residual_blocks(L5, xb_in, n2)

            dve.wait_ge(swa_in, 16 * 6)
            dve.wait_ge(x1_saved, 16)
            m = 0
            for b in range(3):
                n = L6 + b
                split_lo(dve, n + 1, (b + 1) % 2)
                for j in range(4 if b < 2 else 3):
                    th, ct = j // 2, j % 2
                    if b < 2:
                        lo, hi, dst, kj = META + th * HALF, META + (th + 1) * HALF, SQ[:, 2 * b + ct, th * HALF:(th + 1) * HALF], kept[j]
                    else:
                        lo, hi = ((META, META + HALF), (META + HALF, NT), (0, META))[j]
                        dst, kj = SKR[:, lo:hi], (kept[0], kept[2], extra_kept)[j]
                    w = hi - lo
                    dve.wait_ge(q_rot, m + 1)
                    dve.tensor_tensor(PR[m % 2][:, 0:w], bank[4 + m % 2][:, 0:w], psin[:, lo:hi], ALU.mult)
                    raw = NB[j] if b < 2 else (NB[0], NB[2], KMR)[j]
                    dve.tensor_tensor(dst, raw[:, 0:w], pcos[:, lo:hi], ALU.mult)
                    dve.drain()
                    dve.tensor_tensor(dst, dst, PR[m % 2][:, 0:w], ALU.add).then_inc(kj, 1)
                    m += 1

            def window_front(E):
                n, g, u = E // 2, E % 2, E % 3
                lo = P if n == 0 else 0
                dve.wait_ge(s_done, E + 1)
                if E >= 3:
                    dve.wait_ge(t_done, E - 2)
                dve.tensor_tensor(SS[u][:, :, lo:], ps[:, 0:4, lo:KEYS], window[:, lo:].unsqueeze(1).broadcast_to([P, 4, KEYS - lo]), ALU.add).then_inc(s_copied, 1)
                dve.wait_ge(s_copied, E + 1)
                dve.tensor_reduce(SM[:, u, 0, :], SS[u][:, :, lo:], AX.X, ALU.max)
                dve.drain()
                dve.tensor_tensor(SM[:, u, 0, :], SM[:, u, 0, :], sinks[:, 4 * g:4 * g + 4], ALU.max)
                dve.drain()
                dve.tensor_tensor(SM[:, u, 2, :], sinks[:, 4 * g:4 * g + 4], SM[:, u, 0, :], ALU.subtract)
                dve.tensor_scalar(SM[:, u, 0, :], SM[:, u, 0, :], -1.0, None, ALU.mult)
                dve.drain().then_inc(s_max, 1)

            def window_back(E):
                u = E % 3
                lo = P if E < 2 else 0
                dve.wait_ge(s_exp, E + 1)
                dve.tensor_tensor(SM[:, u, 3, :], SM[:, u, 1, :], SM[:, u, 2, :], ALU.add)
                dve.drain()
                dve.reciprocal(SM[:, u, 3, :], SM[:, u, 3, :])
                dve.drain()
                dve.tensor_tensor(SS[u][:, :, lo:], SS[u][:, :, lo:], SM[:, u, 3, :].unsqueeze(2).broadcast_to([P, 4, KEYS - lo]), ALU.mult).then_inc(p_ready, 1)

            def window_keep_pt(E):
                dve.wait_ge(t_done, E + 1)
                dve.tensor_copy(PT[E % 2][1][:, :], bank[5]).then_inc(pt_d, 1)

            def window_keep_out(E):
                n, g = E // 2, E % 2
                dve.wait_ge(so_done, E + 1)
                dve.tensor_copy(OUT[:, 4 + 2 * g:6 + 2 * g, n * P:(n + 1) * P], bank[7][:, 0:2 * P].rearrange("p (a c) -> p a c", a=2)).then_inc(so_kept, 1)

            dve.wait_ge(sk_ok, 6)
            window_front(0)
            window_front(1)
            window_back(0)
            for E in range(16):
                if E < 14:
                    window_front(E + 2)
                window_keep_pt(E)
                if E < 15:
                    window_back(E + 1)
                if E >= 1:
                    window_keep_out(E - 1)
            window_keep_out(15)

            for b in range(3):
                split_lo(dve, L6 + 4 + b, b % 2)
            dve.tensor_scalar(GD[:, 0:2], cols[:, COLS["gate_b"]:COLS["gate_b"] + 2], -1.0, -CLAMP, ALU.mult, ALU.add)
            dve.wait_ge(gla_in, 48)
            pieces = [(c, lo, hi) for c in range(2) for lo, hi in ((META, META + HALF), (META + HALF, NT), (0, META))]

            def gate_clamp(m):
                c, lo, hi = pieces[m]
                dve.wait_ge(gx_done, m + 1)
                dve.tensor_scalar(GB[:, c, lo:hi], bank[4 + m % 2][:, 0:hi - lo], cols[:, COLS["gate_b"] + c:COLS["gate_b"] + c + 1], -CLAMP,
                                  ALU.add, ALU.max).then_inc(gx_clamped, 1)

            dve.wait_ge(gp_done, done(L6 + 5, 1))
            for j in (2, 3):
                dve.sem_inc(kept[j], 1)
            gate_clamp(0)
            for m, (c, lo, hi) in enumerate(pieces):
                if m < 5:
                    gate_clamp(m + 1)
                dve.wait_ge(gx_l, m + 1)
                dve.tensor_tensor(GB[:, c, lo:hi], GB[:, c, lo:hi], GT[m % 2][:, 0:hi - lo], ALU.add).then_inc(gx_r, 1)
            dve.wait_ge(gx_r, 6)
            for c in range(2):
                dve.tensor_tensor_scan(GE[:, :], restart[:, :], GB[:, c, META:NT], 0.0, ALU.mult, ALU.add)
                dve.tensor_tensor_scan(KEM[:, :], restart[:, 1:1 + META], GB[:, c, 0:META], 0.0, ALU.mult, ALU.add)
                dve.drain()
                dve.tensor_copy(GB[:, c, META:NT], GE[:, :])
                dve.tensor_copy(GB[:, c, 0:META], KEM[:, :])
                dve.drain()
            NL = len(GLA_LEVELS)

            def from_ref(p, w):
                b = GB[:, p, META:NT].rearrange("p (n w) -> p n w", w=2 * w)
                dve.tensor_tensor(GE[:, :].rearrange("p (n w) -> p n w", w=2 * w), b, b[:, :, w - 1:w].broadcast_to([P, SEQ // (2 * w), 2 * w]),
                                  ALU.subtract).then_inc(ge_sub, 1)

            def level_operands(p, v):
                dve.wait_ge(ge_exp, 9 * p + v + 1)
                if v >= 2:
                    dve.wait_ge(lv_done, 16 * p + 2 * v - 2)
                if p and v == 1:
                    dve.wait_ge(go_kept, 4)
                dve.tensor_tensor(QE[v % 2][:, :], GQ[:, p, :], GE[:, :], ALU.mult)
                dve.tensor_tensor(KE[v % 2][:, :], GK[:, p, META:NT], GE[:, :], ALU.mult).then_inc(qk_ok, 1)
                dve.wait_ge(qk_ok, 7 * p + v + 1)
                if v < NL - 2:
                    from_ref(p, GLA_LEVELS[v + 1])
                else:
                    dve.drain().then_inc(ge_sub, 1)

            mixed = []

            def mix_lo(th, g):
                mixed.append((th, g))
                k, c = MIX_GROUPS[g], slice(META + th * HALF, META + (th + 1) * HALF)
                dve.wait_ge(c_hi, len(mixed))
                dve.tensor_tensor(A_lo[:, k, c], OUT[:, k, th * HALF:(th + 1) * HALF], A_hi[:, k, c].bitcast(f32),
                                  ALU.subtract).then_inc(c_lo, 1)

            from_ref(0, GLA_LEVELS[0])
            split_lo(dve, L6 + 7, 1)
            level_operands(0, 0)
            split_lo(dve, L6 + 8, 0)
            dve.wait_ge(aa_zero, 1)
            for p in range(2):
                for v in range(1, NL - 1):
                    level_operands(p, v)
                    if p == 0 or v > 1:
                        level_keep(dve, p, v - 1)
                    if v == 5:
                        split_lo(dve, L6 + 9 + p, (p + 1) % 2)
                dve.wait_ge(ge_exp, 9 * p + NL)
                dve.tensor_tensor(QE[1][:, :], GQ[:, p, :], GE[:, :], ALU.mult)
                dve.tensor_tensor(KEM[:, :], GB[:, p, 0:META], GB[:, p, META - 1:META].broadcast_to([P, META]), ALU.subtract)
                dve.drain()
                b = GB[:, p, META:NT].rearrange("p (n w) -> p n w", w=P)
                dve.tensor_tensor(GE[:, :].rearrange("p (n w) -> p n w", w=P), b, b[:, :, P - 1:P].broadcast_to([P, TT, P]),
                                  ALU.subtract).then_inc(ge_sub, 1)
                level_keep(dve, p, NL - 2)
                dve.wait_ge(ge_exp, 9 * p + NL + 1)
                dve.tensor_tensor(KEM[:, :], GK[:, p, 0:META], KEM[:, :], ALU.mult)
                dve.tensor_tensor(KE[1][:, :], GK[:, p, META:NT], GE[:, :], ALU.mult)
                dve.drain().then_inc(qe_ok2, 1)
                if p == 0:
                    from_ref(1, GLA_LEVELS[0])
                level_keep(dve, p, NL - 1)
                for t in range(TT):
                    dve.wait_ge(u_done, 8 * p + t + 1)
                    if t >= 2:
                        dve.wait_ge(go_done, 8 * p + t - 1)
                    if t == 0:
                        dve.tensor_copy(GS[0][:, :], bank[2 + t % 2][:, 0:256]).then_inc(st_ok, 1)
                    else:
                        dve.scalar_tensor_tensor(GS[t % 2][:, :], GS[(t - 1) % 2][:, :], GD[:, 1 + t:2 + t], bank[2 + t % 2][:, 0:256],
                                                 ALU.mult, ALU.add).then_inc(st_ok, 1)
                    dve.wait_ge(st_ok, 8 * p + t + 1)
                if p == 0:
                    level_operands(1, 0)
                    dve.wait_ge(aa_zero, 2)
                    level_keep(dve, 1, 0)
                if p:
                    mix_lo(0, 0)
                    mix_lo(0, 1)
                for j in range(4):
                    dve.wait_ge(gn.rs, 4 * p + j + 1)
                    dve.scalar_tensor_tensor(NB[j][:, :], bank[4 + j], cols[:, COLS["gla_gain"]:COLS["gla_gain"] + 1], NB[j][:, :],
                                             ALU.mult, ALU.mult)
                dve.drain()
                for th in range(2):
                    dve.wait_ge(mg_ok, 1 if p == 0 else 2 + th)
                    for h in range(2):
                        dst = OUT[:, 2 * p + h, th * HALF:(th + 1) * HALF]
                        dve.tensor_tensor(as_gate(p, dst), as_gate(p, NB[2 * h + th][:, :]), mix_gate(p, 2 * th + h), ALU.mult).then_inc(go_kept, 1)
                    if th == 0:
                        for j in range(4):
                            dve.sem_inc(kept[j], 1)
                        if p:
                            mix_lo(0, 2)
            for g in range(3):
                mix_lo(1, g)
            residual_blocks(L7, x1_in, n3)

            def ff_turn(i, last):
                n = L8 + 8 * i
                for b in range(4):
                    split_lo(dve, n + b + 1, (b + 1) % 2)
                    for j in range(4):
                        th, ct = j // 2, j % 2
                        dve.wait_ge(f_hi, 16 * i + 4 * b + j + 1)
                        dve.tensor_tensor(FS[j % 2][:, :], NB[j][:, :], NB[j][:, :], ALU.mult)
                        dve.drain()
                        dve.tensor_tensor(F_lo[:, 2 * b + ct, th * HALF:(th + 1) * HALF], FS[j % 2][:, :],
                                          F_hi[:, 2 * b + ct, th * HALF:(th + 1) * HALF].bitcast(f32), ALU.subtract).then_inc(kept[j], 1)
                for b in range(4):
                    if not last or b < 3:
                        split_lo(dve, n + 4 + b + 1, (b + 1) % 2)
                    for j in range(4):
                        dve.wait_ge(gp_done, done(n + 4 + b, j))
                        h = X1[:, 2 * j:2 * j + 2, b * BC:(b + 1) * BC]
                        dve.tensor_tensor(h, bank[j].rearrange("p (a c) -> p a c", a=2), h, ALU.add).then_inc(kept[j], 1)
                        if last and b == 3 and j:
                            final_scale(2 * j - 2)
                            final_scale(2 * j - 1)

            def final_scale(t):
                if t == 0:
                    dve.wait_ge(fin_gain, 16)
                dve.wait_ge(fin_rstd, t + 1)
                dve.scalar_tensor_tensor(YB[t % 4][:, :], X1[:, t, :], stats[:, t:t + 1], GF[:, :], ALU.mult, ALU.mult).then_inc(fin_ok, 1)

            with dve.Fori(0, 3) as i:
                ff_turn(i, False)
            ff_turn(3, True)
            final_scale(6)
            final_scale(7)

        @block.tensor
        def _(pe):
            pe.wait_ge(const_in, 16 * (1 + len(spec)))
            pe.transpose(bank[7][:, 0:NROWS], rows[0:NROWS, :], ident[0:NROWS, 0:NROWS]).then_inc(const_ok, 1)
            pe.wait_ge(const_ok, 3)
            pe.sem_inc(gp_done, CREDIT)
            n1.pe(pe)
            pe.wait_ge(n1.lo, 8)
            pe.wait_ge(causal_in, 16)

            with pe.Fori(0, 4) as i:
                n = L1 + 4 * i

                def head_sums(m):
                    pe.wait_ge(hn.sq, 8 * i + m + 1)
                    pe.matmul(bank[4 + m % 2], ones[:, :], NB[m % 4][:, :], start=True, stop=True).then_inc(hn.ss, 1)

                gemm(pe, n, 0, A_hi, A_lo, False, between=lambda j: j and head_sums(j - 1))
                gemm(pe, n + 1, 1, A_hi, A_lo, False, between=lambda j: head_sums(j + 3))
                gemm(pe, n + 2, 0, A_hi, A_lo, True, between=lambda j: j == 0 and head_sums(7))
                for j in range(4):
                    pe.wait_ge(kept[j], kept_by(n + 2))

                def scores(S):
                    c, qt = step(S)
                    w = step_w(S)
                    if S >= 2:
                        pe.wait_ge(z_used, 16 * i + S - 1)
                    for h in range(0, w, HALF):
                        e = min(w, h + HALF)
                        z = wide(4 + 2 * (S % 2))[:, h:e]
                        pe.matmul(z, Q[:, c, qt * P:(qt + 1) * P], K[:, c, h:e], start=True, stop=(e < w))
                    z = wide(4 + 2 * (S % 2))[:, w - P:w]
                    pe.matmul(z, ident[:, :], causal[:, :], start=False, stop=True).then_inc(z_done, 1)

                def turn(S):
                    pe.wait_ge(wgt, 16 * i + S + 1)
                    if S >= 1:
                        pe.wait_ge(wt0, 16 * i + S)
                        if long_steps(S):
                            pe.wait_ge(wt1, 8 * i + long_steps(S))
                    for kb in range(step(S)[1] + 1):
                        last = pe.transpose(wide(0)[:, kb * P:(kb + 1) * P], C[S % 2][:, kb * P:(kb + 1) * P], ident[:, :])
                    last.then_inc(tr_done, 1)

                def weigh(q):
                    S, c, m = PAIRS[q]
                    qt = 2 * m + 1
                    pe.wait_ge(wt0, 16 * i + S + 1)
                    if long_steps(S + 1):
                        pe.wait_ge(wt1, 8 * i + long_steps(S + 1))
                    if q >= 1:
                        pe.wait_ge(o_kept, 8 * i + q)
                    for kb in range(qt + 1):
                        lo = P if kb == qt else 0
                        last = pe.matmul(bank[2][:, lo:2 * P], V[:, kb, c * P:(c + 1) * P], WT[c][:, kb, lo:2 * P],
                                         start=(kb == 0), stop=(kb == qt))
                    last.then_inc(pv_done, 1)

                def gate_part(S):
                    for m in range(gate_upto[S - 1] if S else 0, gate_upto[S]):
                        j, r = divmod(m, PASSES)
                        th, ct = j // 2, j % 2
                        k, g = divmod(r, 3)
                        if r == 0 and j == 0:
                            pe.wait_ge(w_lo, n + 4)
                        elif r == 0:
                            pe.wait_ge(g_raw, 4 * i + j)
                        w, a = ((W_hi, A_hi), (W_hi, A_lo), (W_lo, A_hi))[g]
                        last = pe.matmul(bank[3], w[1][:, k, ct * P:(ct + 1) * P], a[:, k, META + th * HALF:META + (th + 1) * HALF],
                                         start=(r == 0), stop=(r == PASSES - 1))
                        if r == PASSES - 1:
                            last.then_inc(gp_done, 1)

                scores(0)
                scores(1)
                for S in range(16):
                    if S - 1 in pair_after:
                        weigh(pair_after[S - 1])
                    if S < 14:
                        scores(S + 2)
                    if S == 0:
                        gate_part(S)
                    turn(S)
                    if S:
                        gate_part(S)
                weigh(7)
                pe.wait_ge(g_raw, 4 * i + 4)

            def branch(b, B):
                with pe.Fori(0, 4) as i:
                    gemm(pe, B + 2 * i, 0, A_hi, A_lo, False)
                    pe.wait_ge(s_lo[b], KT)
                    gemm(pe, B + 2 * i + 1, 1, S_hi, S_lo, False)

            branch(0, B1)
            with pe.Fori(0, 4) as i:
                n = L3 + 4 * i
                gemm(pe, n, 0, A_hi, A_lo, False)
                gemm(pe, n + 1, 1, A_hi, A_lo, False)
                gemm(pe, n + 2, 0, A_hi, A_lo, True)
                pe.wait_ge(rot_ok, 4 * i + 4)
                def scores(kb):
                    w = SEQ - P * kb
                    if kb >= 2:
                        pe.wait_ge(at_ready, 8 * i + kb - 1)
                    for h in range(0, w, HALF):
                        e = min(w, h + HALF)
                        for c in range(2):
                            last = pe.matmul(wide(4 + 2 * (kb % 2))[:, h:e], RK[:, c, kb * P:(kb + 1) * P],
                                             RQ[:, c, kb * P + h:kb * P + e], start=(c == 0), stop=(c == 1))
                    last.then_inc(a_done, 1)

                def weigh(kb):
                    pe.wait_ge(at_ready, 8 * i + kb + 1)
                    for th in range(2):
                        lo, hi = max(th * HALF, kb * P), (th + 1) * HALF
                        if lo >= hi:
                            continue
                        for c in range(2):
                            last = pe.matmul(bank[2 * th + c][:, lo - th * HALF:HALF], RV[:, kb, c * P:(c + 1) * P],
                                             AT[kb % 2][:, lo - kb * P:hi - kb * P], start=(kb == 0), stop=(kb == 4 * th + 3))
                    last.then_inc(rv_part, 1)

                scores(0)
                scores(1)
                for j in range(4):
                    pe.wait_ge(kept[j], kept_by(n + 2))
                for kb in range(TT):
                    weigh(kb)
                    if kb < TT - 2:
                        scores(kb + 2)

                def head_sums(j):
                    if j:
                        return
                    for th in range(2):
                        pe.wait_ge(rn.sq, 4 * i + 2 * th + 2)
                        for c in range(2):
                            last = pe.matmul(bank[4 + th], ones[:, :], NB[2 * th + c][:, :], start=(c == 0), stop=(c == 1))
                        last.then_inc(rn.ss, 1)

                gemm(pe, n + 3, 1, A_hi, A_lo, False, between=head_sums, banks=RET_GATE,
                     before=lambda j: j >= 2 and pe.wait_ge(rn.rs, 2 * i + j - 1))
            branch(1, B2)

            def residual_blocks(B, low, parts, norm, banks_free=None):
                def operand_ready(j):
                    if j % 2 == 0:
                        pe.wait_ge(low, parts[j // 2])
                    if banks_free:
                        banks_free(j)
                gemm(pe, B, 0, A_hi, A_lo, True, before=operand_ready)
                gemm(pe, B + 1, 1, A_hi, A_lo, True)
                gemm(pe, B + 2, 0, A_hi, A_lo, True)
                if norm.m:
                    norm.turn(pe, -1)
                gemm(pe, B + 3, 1, A_hi, A_lo, True, between=lambda j: norm.pe_between(pe, j))

            residual_blocks(L5, m_lo, (8, 10), n2)

            def small(out_ap, parts):
                for k in range(KT):
                    for g, (a, b) in enumerate(parts(k)):
                        last = pe.matmul(out_ap, a, b, start=(k == 0 and g == 0), stop=(k == KT - 1 and g == 2))
                return last

            def meta_rows(out_ap, s, lo):
                c = slice(lo, lo + P)
                return small(out_ap, lambda k: ((W_hi[s][:, k, c], A_hi[:, k, 0:META]), (W_hi[s][:, k, c], A_lo[:, k, 0:META]),
                                                (W_lo[s][:, k, c], A_hi[:, k, 0:META])))

            def meta_tokens(out_ap, s, lo, hi):
                c = slice(lo, hi)
                return small(out_ap, lambda k: ((A_hi[:, k, 0:P], W_hi[s][:, k, c]), (A_hi[:, k, 0:P], W_lo[s][:, k, c]),
                                                (A_lo[:, k, 0:P], W_hi[s][:, k, c])))

            def rope_product(m, src, w=HALF):
                if m < 10:
                    pe.wait_ge(q_raw, m + 1)
                if m >= 2:
                    n_, j_ = divmod(m - 2, 4)
                    pe.wait_ge(kept[j_], kept_by(L6 + n_))
                pe.matmul(bank[4 + m % 2][:, 0:w], rot[:, :], src, start=True, stop=True).then_inc(q_rot, 1)

            def after_norm(norm, j):
                if j % 2 == 0:
                    pe.wait_ge(norm.lo, norm.m + 4 + 2 * j)

            def first_window_rows(j):
                if j == 0:
                    n2.pe_between(pe, 4)
                else:
                    if j == 1:
                        pe.wait_ge(n2.lo, TT + 1)
                        pe.wait_ge(swa_in, 16 * 6)
                    rope_product(j - 1, NB[j - 1][:, :])

            gemm(pe, L6, 0, A_hi, A_lo, False, between=first_window_rows, before=lambda j: after_norm(n2, j))
            gemm(pe, L6 + 1, 1, A_hi, A_lo, False, between=lambda j: rope_product(j + 3, NB[(j + 3) % 4][:, :]))
            n = L6 + 2
            pe.wait_ge(w_lo, n + 1)
            meta_tokens(bank[7][:, 0:BC], 0, 0, BC).then_inc(extra, 1)

            def turn_values(j, b):
                pe.wait_ge(kept[j], kept_by(n))
                for r_ in range(4):
                    last = pe.transpose(bank[b][:, r_ * P:(r_ + 1) * P], NB[j][:, r_ * P:(r_ + 1) * P], ident[:, :])
                last.then_inc(v_turned, 1)

            def window_keys(j):
                if j == 0:
                    rope_product(7, NB[3][:, :])
                elif j == 1:
                    pe.wait_ge(km_ok, 1)
                    pe.transpose(bank[7][:, 0:META], KMT[:, :], ident[0:META, 0:META]).then_inc(km_turned, 1)
                    rope_product(8, NB[0][:, :])
                elif j == 2:
                    turn_values(1, 6)
                else:
                    rope_product(9, NB[2][:, :])

            gemm(pe, n, 0, A_hi, A_lo, False, between=window_keys)
            pe.wait_ge(km_raw, 1)
            rope_product(10, KMR[:, :], META)
            turn_values(3, 7)
            pe.wait_ge(sv_ok, 3)
            pe.wait_ge(extra_kept, 1)
            for j in range(4):
                pe.wait_ge(kept[j], kept_by(L6 + 2))
            for g in range(2):
                for c, (lo, hi) in enumerate(((META, META + HALF), (META + HALF, NT), (0, META))):
                    if 3 * g + c >= 4:
                        pe.wait_ge(sk_ok, 3 * g + c - 3)
                    pe.matmul(bank[(3 * g + c) % 4][:, 0:hi - lo], dup[:, g, :], SKR[:, lo:hi], start=True, stop=True).then_inc(dup_done, 1)
            pe.wait_ge(sk_ok, 6)

            def window_scores(E):
                n, g = E // 2, E % 2
                if E >= 1:
                    pe.wait_ge(s_copied, E)
                for h in range(4):
                    head = 4 * g + h
                    half = slice(64 * (head % 2), 64 * (head % 2) + 64)
                    q = SQ[half, head // 2, n * P:(n + 1) * P]
                    lo = 0 if n else P
                    pe.matmul(bank[h][:, lo:2 * P], q, SK[half, g, META + (n - 1) * P + lo:META + (n + 1) * P], start=True, stop=True)
                    last = pe.matmul(bank[h][:, 2 * P:KEYS], q, SK[half, g, 0:META], start=True, stop=True)
                last.then_inc(s_done, 1)

            def window_turn(E):
                n, u = E // 2, E % 2
                pe.wait_ge(p_ready, E + 1)
                if E >= 1:
                    pe.wait_ge(pt_a, E)
                    pe.wait_ge(pt_d, E)
                u = E % 3
                for h in range(4):
                    at_ = ((h % 2) * 2 + h // 2) * P
                    if n:
                        pe.transpose(bank[4][:, at_:at_ + P], SS[u][:, h, 0:P], ident[:, :])
                    pe.transpose(bank[5][:, at_:at_ + P], SS[u][:, h, P:2 * P], ident[:, :])
                    last = pe.transpose(bank[6][0:META, at_:at_ + P], SS[u][:, h, 2 * P:KEYS], ident[:, :])
                last.then_inc(t_done, 1)

            def window_out(E):
                n, g, u = E // 2, E % 2, E % 2
                pe.wait_ge(pt_a, E + 1)
                pe.wait_ge(pt_d, E + 1)
                if E >= 1:
                    pe.wait_ge(so_kept, E)
                ops = []
                for odd in range(2):
                    c, v = slice(odd * 2 * P, (odd + 1) * 2 * P), slice(64 * (1 - odd), 64 * (1 - odd) + P)
                    if n:
                        ops.append((SV[:, n - 1, g, v], PT[u][0][:, c]))
                    ops.append((SV[:, n, g, v], PT[u][1][:, c]))
                    ops.append((SVM[:, g, v], PT[u][2][0:META, c]))
                for m, (a, b) in enumerate(ops):
                    last = pe.matmul(bank[7][:, 0:2 * P], a, b, start=(m == 0), stop=(m == len(ops) - 1))
                last.then_inc(so_done, 1)

            window_scores(0)
            window_scores(1)
            for E in range(16):
                if E < 14:
                    window_scores(E + 2)
                window_turn(E)
                if E >= 1:
                    window_out(E - 1)
            window_out(15)

            pe.wait_ge(so_kept, 16)
            gemm(pe, L6 + 3, 1, A_hi, A_lo, False)
            pe.wait_ge(w_lo, L6 + 5)
            meta_rows(bank[6][:, 0:META], 0, 0)
            meta_rows(bank[6][:, META:2 * META], 0, P).then_inc(extra, 1)
            gemm(pe, L6 + 4, 0, A_hi, A_lo, False)
            n, s = L6 + 5, 1
            pe.wait_ge(extra, 2)
            pe.wait_ge(w_lo, n + 1)
            for j in range(2):
                pe.wait_ge(kept[j], n + 1)
                t = slice(META + j * HALF, META + (j + 1) * HALF)
                last = small(bank[j], lambda k: ((W_hi[s][:, k, 0:P], A_hi[:, k, t]), (W_hi[s][:, k, 0:P], A_lo[:, k, t]),
                                                 (W_lo[s][:, k, 0:P], A_hi[:, k, t])))
                if j == 0:
                    last.then_inc(gp_done, 1)
            last.then_inc(gp_done, 1)
            pe.wait_ge(extra_kept, 2)
            meta_rows(bank[6][:, 0:META], s, 0).then_inc(extra, 1)
            pe.wait_ge(extra, 3)
            pe.sem_inc(gp_done, 2)
            pe.wait_ge(lr_ok, 1)
            pe.wait_ge(kept[0], kept_by(n))
            pe.wait_ge(kept[1], kept_by(n))
            pe.wait_ge(gla_in, 48)
            for m, (c, lo, hi) in enumerate([(c, lo, hi) for c in range(2) for lo, hi in ((META, META + HALF), (META + HALF, NT), (0, META))]):
                if m >= 2:
                    pe.wait_ge(gx_l, m - 1)
                pe.matmul(bank[4 + m % 2][:, 0:hi - lo], wgu[:, c * P:(c + 1) * P], LR[:, lo:hi], start=True, stop=True).then_inc(gx_done, 1)
            for b in range(2):
                if b:
                    pe.wait_ge(extra_kept, 3)
                pe.wait_ge(w_lo, L6 + 7 + b)
                meta_tokens(bank[7][:, 0:BC], b, 0, BC).then_inc(extra, 1)
                gemm(pe, L6 + 6 + b, b, A_hi, A_lo, True)
            pe.wait_ge(extra_kept, 4)
            for j in range(4):
                pe.wait_ge(kept[j], kept_by(L6 + 7))
            NL = len(GLA_LEVELS)

            def level(p, v):
                if v < NL - 1:
                    pe.wait_ge(qk_ok, 7 * p + v + 1)
                for h in range(2):
                    U = 2 * v + h
                    if U >= 3:
                        pe.wait_ge(lv_kept, 16 * p + U - 2)
                    half = slice(64 * h, 64 * h + 64)
                    for t in range(TT):
                        if v < NL - 1:
                            a, b = KE[v % 2][half, t * P:(t + 1) * P], QE[v % 2][half, t * P:(t + 1) * P]
                        else:
                            a, b = GK[half, p, META + t * P:META + (t + 1) * P], GQ[half, p, t * P:(t + 1) * P]
                        last = pe.matmul(bank[2 * (U % 3) + t // 4][:, (t % 4) * P:(t % 4 + 1) * P], a, b, start=True, stop=True)
                    last.then_inc(lv_done, 1)

            def mix_gate_part(p, first, last_):
                for m in range(first, last_):
                    j, r_ = divmod(m, PASSES)
                    th, ct = j // 2, j % 2
                    k, g = divmod(r_, 3)
                    if m == 0:
                        pe.wait_ge(w_lo, L6 + 9 + p)
                    elif r_ == 0 and (p == 0 or j == 1):
                        pe.wait_ge(mg_raw, 4 * p + max(j - 1, 1))
                    w, a = ((W_hi, A_hi), (W_hi, A_lo), (W_lo, A_hi))[g]
                    b = j % 2 if p and j >= 2 else 6 + j % 2
                    o = pe.matmul(bank[b], w[p][:, k, ct * P:(ct + 1) * P], a[:, k, META + th * HALF:META + (th + 1) * HALF],
                                  start=(r_ == 0), stop=(r_ == PASSES - 1))
                    if r_ == PASSES - 1:
                        o.then_inc(gp_done, 1)

            def level_and_gate(p, v):
                level(p, v)
                mix_gate_part(p, mix_upto[p][v - 1] if v else 0, mix_upto[p][v])

            def gla_sums(p, j):
                pe.wait_ge(gn.sq, 4 * p + j + 1)
                if j >= 2:
                    pe.wait_ge(gn.rs, 4 * p + j - 1)
                pe.matmul(bank[2 + j % 2], ones[:, :], NB[j][:, :], start=True, stop=True).then_inc(gn.ss, 1)

            level_and_gate(0, 0)
            for p in range(2):
                if p:
                    pe.wait_ge(go_kept, 4)
                for v in range(1, NL):
                    level_and_gate(p, v)
                pe.wait_ge(lv_kept, 16 * p + 2 * NL - 2)
                pe.wait_ge(mg_raw, (4, 6)[p])
                pe.wait_ge(qe_ok2, p + 1)
                for t in range(TT):
                    pe.transpose(wide(6)[:, t * P:(t + 1) * P], KE[1][:, t * P:(t + 1) * P], ident[:, :])
                pe.transpose(bank[2][0:META, 0:P], KEM[:, :], ident[:, :]).then_inc(kt_done, 1)
                pe.wait_ge(kt_ok, p + 1)

                def update(t):
                    if t >= 2:
                        pe.wait_ge(st_ok, 8 * p + t - 1)
                    if t == 0:
                        pe.matmul(bank[2][:, 0:256], KTM[:, :], GVM[:, p * 256:(p + 1) * 256], start=True, stop=True).then_inc(u_done, 1)
                    else:
                        pe.matmul(bank[2 + t % 2][:, 0:256], KTK[:, t - 1, :], GV[:, t - 1, p * 256:(p + 1) * 256], start=True, stop=True).then_inc(u_done, 1)

                update(0)
                for t in range(TT):
                    if t < TT - 1:
                        update(t + 1)
                    pe.wait_ge(st_ok, 8 * p + t + 1)
                    if t == 0:
                        pe.wait_ge(lv_kept, 16 * p + 2 * NL)
                    for h in range(2):
                        half = slice(64 * h, 64 * h + 64)
                        o = bank[4 + 2 * h + t // 4][:, (t % 4) * P:(t % 4 + 1) * P]
                        pe.matmul(o, GV[:, t, (2 * p + h) * P:(2 * p + h + 1) * P], AA[:, TT * h + t, :], start=True, stop=False)
                        last = pe.matmul(o, GS[t % 2][half, h * P:(h + 1) * P], QE[1][half, t * P:(t + 1) * P], start=False, stop=True)
                    last.then_inc(go_done, 1)
                if p == 0:
                    pe.wait_ge(st_ok, TT)
                    level(1, 0)
                    pe.wait_ge(lv_kept, 2 * NL + 2)
                    for j in range(4):
                        gla_sums(0, j)

            mix_gate_part(1, 2 * PASSES, 3 * PASSES)
            gla_sums(1, 0)
            gla_sums(1, 1)
            mix_gate_part(1, 3 * PASSES, 3 * PASSES + PASSES // 2)
            gla_sums(1, 2)
            gla_sums(1, 3)
            mix_gate_part(1, 3 * PASSES + PASSES // 2, 4 * PASSES)
            pe.wait_ge(mg_raw, 7)

            def mix_banks_free(j):
                if j == 1:
                    pe.wait_ge(mg_raw, 8)
                if j == 2:
                    pe.wait_ge(gn.rs, 8)
            residual_blocks(L7, c_lo, (3, 6), n3, mix_banks_free)

            def ff_turn(i, first):
                n = L8 + 8 * i
                for b in range(4):
                    if first and b == 0:
                        gemm(pe, n, 0, A_hi, A_lo, False, between=lambda j: j == 0 and n3.pe_between(pe, 4),
                             before=lambda j: after_norm(n3, j))
                    else:
                        gemm(pe, n + b, b % 2, A_hi, A_lo, False)

                def hidden_ready(j):
                    if j % 2 == 0:
                        pe.wait_ge(kept[j + 1], kept_by(n + 3))
                for b in range(4):
                    gemm(pe, n + 4 + b, b % 2, F_hi, F_lo, True, before=hidden_ready if b == 0 else None)

            ff_turn(0, True)
            with pe.Fori(1, 4) as i:
                ff_turn(i, False)


_INS = ["x", "norm_gain", "w_in", "b_merge", "sb_q_gain", "sb_k_gain", "ret_out_gain", "w_branch_sb", "w_branch_ret", "w_out",
        "meta_tokens_2", "norm_mix_w_2", "w_in_2", "w_gate_up_2", "b_gate_2", "gla_norm_w_2", "sinks_2", "w_out_2",
        "norm_ff_w_2", "w_ff1_2", "w_ff2_2", "final_norm_w_2"]


def kernel(**inputs):
    import concourse.bacc as bacc
    from concourse.bass_utils import run_bass_kernel_spmd

    nc = bacc.Bacc("TRN2", target_bir_lowering=False, num_devices=1)
    arrays, args, tab = {}, {}, {}
    for name in _INS:
        a = np.ascontiguousarray(inputs[name])
        arrays["in_" + name] = a
        args[name] = nc.dram_tensor("in_" + name, a.shape, mybir.dt.from_np(a.dtype), kind="ExternalInput").ap()
    for name, a in shape_tables().items():
        arrays["tab_" + name] = a
        tab[name] = nc.dram_tensor("tab_" + name, a.shape, mybir.dt.from_np(a.dtype), kind="ExternalInput").ap()
    out = nc.dram_tensor("out", (1, SEQ, DM), mybir.dt.float32, kind="ExternalOutput").ap()
    build(nc, tab=tab, out=out, **args)
    r = run_bass_kernel_spmd(nc, [arrays], core_ids=[0])
    return r.results[0]["out"]
```
